# Optimizing a Trainium2 kernel written in Bass

```python
import math
import jax, jax.numpy as jnp
from jax import lax
import numpy as np

D_MODEL = 1024
BATCH = 1
SEQ = 512
DEPTH = 2

HEAD_DIM = 128
RET_HEADS = D_MODEL // (2 * HEAD_DIM)
RET_DK = HEAD_DIM
RET_DV = HEAD_DIM
HGRN_HEADS = D_MODEL // (2 * HEAD_DIM)
HGRN_DK = HEAD_DIM
HGRN_DV = HEAD_DIM
RET_WIDTH = RET_HEADS * RET_DV
HGRN_WIDTH = HGRN_HEADS * HGRN_DV
MIX_WIDTH = RET_WIDTH + HGRN_WIDTH
RET_QK_W = RET_HEADS * RET_DK
HGRN_QK_W = HGRN_HEADS * HGRN_DK
SPLIT_SIZES = (RET_QK_W, RET_QK_W, RET_WIDTH, RET_WIDTH,
               HGRN_QK_W, HGRN_QK_W, HGRN_WIDTH, HGRN_WIDTH)
IN_COLS = sum(SPLIT_SIZES)
D_FF = 2816
CONV_WIDTH = 3
CHUNK = 64
ROPE_BASE = 10000.0
EPS = 1e-6
N_MOD = 6


def rms_norm(x, w):
    xf = x.astype(jnp.float32)
    y = xf * lax.rsqrt(jnp.mean(xf * xf, axis=-1, keepdims=True) + EPS)
    return (y * w.astype(jnp.float32)).astype(x.dtype)

def head_norm(o, w):
    H, D = o.shape[-2], o.shape[-1]
    y = o * lax.rsqrt(jnp.mean(o * o, axis=-1, keepdims=True) + EPS)
    return y * w.astype(jnp.float32).reshape(H, D)

def rotary(x, cos, sin):
    x1, x2 = jnp.split(x, 2, axis=-1)
    c = cos[None, :, None, :]
    s = sin[None, :, None, :]
    return jnp.concatenate([x1 * c - x2 * s, x1 * s + x2 * c], axis=-1)

def to_chunks(t):
    B, S, H, D = t.shape
    n = S // CHUNK
    return t.astype(jnp.float32).reshape(B, n, CHUNK, H, D).transpose(1, 0, 3, 2, 4)

def from_chunks(t):
    n, B, H, C, D = t.shape
    return t.transpose(1, 0, 3, 2, 4).reshape(B, n * C, H, D)

def retention_chunkwise(q, k, v, log_gamma):
    qc, kc, vc = to_chunks(q), to_chunks(k), to_chunks(v)
    B, H, DK, DV = qc.shape[1], qc.shape[2], qc.shape[4], vc.shape[4]
    pos = jnp.arange(CHUNK, dtype=jnp.float32)
    lg = log_gamma.astype(jnp.float32)[:, None]
    rel = pos[:, None] - pos[None, :]
    decay_mask = jnp.where(rel[None] >= 0, jnp.exp(lg[:, :, None] * jnp.maximum(rel, 0.0)[None]), 0.0)
    q_decay = jnp.exp(lg * (pos + 1.0))[None, :, :, None]
    k_decay = jnp.exp(lg * (CHUNK - 1.0 - pos))[None, :, :, None]
    chunk_decay = jnp.exp(lg[:, 0] * CHUNK)[None, :, None, None]

    def step(state, inp):
        qi, ki, vi = inp
        scores = jnp.einsum('bhid,bhjd->bhij', qi, ki) * decay_mask[None]
        intra = jnp.einsum('bhij,bhjv->bhiv', scores, vi)
        inter = jnp.einsum('bhid,bhdv->bhiv', qi, state) * q_decay
        new_state = state * chunk_decay + jnp.einsum('bhjd,bhjv->bhdv', ki * k_decay, vi)
        return new_state, intra + inter

    init = jnp.zeros((B, H, DK, DV), jnp.float32)
    _, out = lax.scan(step, init, (qc, kc, vc))
    return from_chunks(out)

def hgrn2_chunkwise(q, log_f, k, v):
    qc, lfc, kc, vc = to_chunks(q), to_chunks(log_f), to_chunks(k), to_chunks(v)
    B, H, DK, DV = qc.shape[1], qc.shape[2], qc.shape[4], vc.shape[4]
    causal = jnp.tril(jnp.ones((CHUNK, CHUNK), dtype=bool))[:, :, None]

    def step(state, inp):
        qi, lfi, ki, vi = inp
        b = jnp.cumsum(lfi, axis=-2)
        diff = b[:, :, :, None, :] - b[:, :, None, :, :]
        decay = jnp.where(causal, jnp.exp(jnp.where(causal, diff, 0.0)), 0.0)
        scores = jnp.sum(qi[:, :, :, None, :] * ki[:, :, None, :, :] * decay, axis=-1)
        intra = jnp.einsum('bhij,bhjv->bhiv', scores, vi)
        inter = jnp.einsum('bhid,bhdv->bhiv', qi * jnp.exp(b), state)
        b_last = b[:, :, -1:, :]
        new_state = state * jnp.exp(b_last)[:, :, 0, :, None] + jnp.einsum('bhjd,bhjv->bhdv', ki * jnp.exp(b_last - b), vi)
        return new_state, intra + inter

    init = jnp.zeros((B, H, DK, DV), jnp.float32)
    _, out = lax.scan(step, init, (qc, lfc, kc, vc))
    return from_chunks(out)

def hybrid_mixer(h, w_in, w_out, ret_norm_w, hgrn_norm_w, lb, cos, sin, log_gamma):
    B, S, _ = h.shape
    proj = h @ w_in
    idx = np.cumsum(SPLIT_SIZES)[:-1].tolist()
    rq, rk, rv, rg, hq, hf, hi, hg = jnp.split(proj, idx, axis=-1)

    rq = rotary(rq.reshape(B, S, RET_HEADS, RET_DK).astype(jnp.float32), cos, sin)
    rk = rotary(rk.reshape(B, S, RET_HEADS, RET_DK).astype(jnp.float32), cos, sin) * (RET_DK ** -0.5)
    rv = rv.reshape(B, S, RET_HEADS, RET_DV)
    r_out = retention_chunkwise(rq, rk, rv, log_gamma)
    r_out = head_norm(r_out, ret_norm_w) * jax.nn.silu(rg.astype(jnp.float32).reshape(B, S, RET_HEADS, RET_DV))

    z = hf.astype(jnp.float32).reshape(B, S, HGRN_HEADS, HGRN_DK)
    lbh = lb.astype(jnp.float32).reshape(HGRN_HEADS, HGRN_DK)
    log_f = jax.nn.log_sigmoid(z) + jnp.log1p(lbh * jnp.exp(-z))
    k_in = (1.0 - lbh) * jax.nn.sigmoid(-z)
    q_h = jax.nn.silu(hq.astype(jnp.float32).reshape(B, S, HGRN_HEADS, HGRN_DK))
    v_h = hi.reshape(B, S, HGRN_HEADS, HGRN_DV)
    g_out = hgrn2_chunkwise(q_h, log_f, k_in, v_h)
    g_out = head_norm(g_out, hgrn_norm_w) * jax.nn.silu(hg.astype(jnp.float32).reshape(B, S, HGRN_HEADS, HGRN_DV))

    merged = jnp.concatenate([r_out.reshape(B, S, RET_WIDTH), g_out.reshape(B, S, HGRN_WIDTH)], axis=-1)
    return merged.astype(h.dtype) @ w_out

def conv_ffn(h, w_gate, w_val, conv_w, conv_b, w_down):
    a = h @ w_gate
    S = a.shape[1]
    ap = jnp.pad(a, ((0, 0), (CONV_WIDTH - 1, 0), (0, 0)))
    acc = conv_b[None, None, :] + ap[:, 0:S] * conv_w[0]
    for j in range(1, CONV_WIDTH):
        acc = acc + ap[:, j:j + S] * conv_w[j]
    return (jax.nn.silu(acc) * (h @ w_val)) @ w_down

def first_inputs(seed: int = 0) -> dict:
    key = jax.random.key(seed)
    ks = jax.random.split(key, 20)
    f32 = jnp.float32
    nrm = lambda k, shape, s: (jax.random.normal(k, shape, f32) * s).astype(f32)
    return {
        'x': nrm(ks[0], (BATCH, SEQ, D_MODEL), 1.0),
        'c': nrm(ks[1], (BATCH, D_MODEL), 1.0),
        'w_in': nrm(ks[2], (DEPTH, D_MODEL, IN_COLS), D_MODEL ** -0.5),
        'w_out': nrm(ks[3], (DEPTH, MIX_WIDTH, D_MODEL), MIX_WIDTH ** -0.5),
        'ret_norm_w': 1.0 + nrm(ks[4], (DEPTH, RET_WIDTH), 0.02),
        'hgrn_norm_w': 1.0 + nrm(ks[5], (DEPTH, HGRN_WIDTH), 0.02),
        'hgrn_lb_logits': nrm(ks[6], (DEPTH, HGRN_HEADS * HGRN_DK), 0.1),
        'norm1_w': 1.0 + nrm(ks[7], (DEPTH, D_MODEL), 0.02),
        'norm2_w': 1.0 + nrm(ks[8], (DEPTH, D_MODEL), 0.02),
        'ada_w': nrm(ks[9], (DEPTH, D_MODEL, N_MOD * D_MODEL), 0.5 * D_MODEL ** -0.5),
        'ada_b': nrm(ks[10], (DEPTH, N_MOD * D_MODEL), 0.01),
        'w_gate': nrm(ks[11], (DEPTH, D_MODEL, D_FF), D_MODEL ** -0.5),
        'w_val': nrm(ks[12], (DEPTH, D_MODEL, D_FF), D_MODEL ** -0.5),
        'conv_w': nrm(ks[13], (DEPTH, CONV_WIDTH, D_FF), CONV_WIDTH ** -0.5),
        'conv_b': nrm(ks[14], (DEPTH, D_FF), 0.01),
        'w_down': nrm(ks[15], (DEPTH, D_FF, D_MODEL), D_FF ** -0.5),
        'final_norm_w': 1.0 + nrm(ks[16], (D_MODEL,), 0.02),
    }

def first_block(x, c, w_in, w_out, ret_norm_w, hgrn_norm_w, hgrn_lb_logits, norm1_w, norm2_w,
              ada_w, ada_b, w_gate, w_val, conv_w, conv_b, w_down, final_norm_w):
    S = x.shape[1]
    pos = jnp.arange(S, dtype=jnp.float32)
    inv_freq = ROPE_BASE ** (-jnp.arange(0, RET_DK, 2, dtype=jnp.float32) / RET_DK)
    ang = pos[:, None] * inv_freq[None, :]
    cos, sin = jnp.cos(ang), jnp.sin(ang)
    log_gamma = jnp.log(1.0 - jnp.exp2(-5.0 - jnp.arange(RET_HEADS, dtype=jnp.float32)))
    p = jax.nn.softmax(hgrn_lb_logits.astype(jnp.float32), axis=0)
    lower_bounds = jnp.cumsum(p, axis=0) - p[0:1]
    c_act = jax.nn.silu(c)

    for l in range(DEPTH):
        mod = (c_act @ ada_w[l] + ada_b[l])[:, None, :]
        sh1, sc1, g1, sh2, sc2, g2 = jnp.split(mod, N_MOD, axis=-1)
        h = rms_norm(x, norm1_w[l]) * (1.0 + sc1) + sh1
        x = x + g1 * hybrid_mixer(h, w_in[l], w_out[l], ret_norm_w[l], hgrn_norm_w[l],
                                  lower_bounds[l], cos, sin, log_gamma)
        h = rms_norm(x, norm2_w[l]) * (1.0 + sc2) + sh2
        x = x + g2 * conv_ffn(h, w_gate[l], w_val[l], conv_w[l], conv_b[l], w_down[l])

    return rms_norm(x, final_norm_w)


PLE_DIM = 256
HEAD_DIM_2 = 64
N_Q_HEADS = 16
N_KV_HEADS = 4
Q_PER_KV = N_Q_HEADS // N_KV_HEADS
WINDOW = 128
BLOCK = 128
ROPE_THETA = 10000.0
ATT_Q = N_Q_HEADS * HEAD_DIM_2
ATT_KV = N_KV_HEADS * HEAD_DIM_2
RW_HEADS = 16
RW_HEAD = 64
RW_DIM = RW_HEADS * RW_HEAD
DECAY_RANK = 64
ICLR_RANK = 64
GATE_RANK = 160
RW_SHIFT_COLS = 3 * RW_DIM + DECAY_RANK + ICLR_RANK + GATE_RANK
D_IN = ATT_Q + 2 * ATT_KV + RW_SHIFT_COLS + 2 * D_MODEL
FFN_DIM = 2816
CONV_W = 3
NORM_EPS = 1e-6
GN_EPS = 64e-5


def _split(z, sizes):
    out, off = [], 0
    for s in sizes:
        out.append(z[..., off:off + s])
        off += s
    return out

def rmsnorm(x, g):
    xf = x.astype(jnp.float32)
    y = xf * lax.rsqrt(jnp.mean(xf * xf, axis=-1, keepdims=True) + NORM_EPS)
    return (y * g.astype(jnp.float32)).astype(x.dtype)

def rope(t, positions):
    half = HEAD_DIM_2 // 2
    inv_freq = jnp.power(ROPE_THETA, -jnp.arange(half, dtype=jnp.float32) / half)
    ang = positions.astype(jnp.float32)[..., None] * inv_freq
    cos = jnp.cos(ang)[:, :, None, :]
    sin = jnp.sin(ang)[:, :, None, :]
    tf = t.astype(jnp.float32)
    t1, t2 = tf[..., :half], tf[..., half:]
    return jnp.concatenate([t1 * cos - t2 * sin, t2 * cos + t1 * sin], axis=-1).astype(t.dtype)

def sliding_window_attention(q, k, v, sinks):
    B, S = q.shape[0], q.shape[1]
    nb = S // BLOCK
    qb = q.astype(jnp.float32).reshape(B, nb, BLOCK, N_KV_HEADS, Q_PER_KV, HEAD_DIM_2)

    def kv_blocks(t):
        t = t.astype(jnp.float32)
        prev = jnp.pad(t, ((0, 0), (BLOCK, 0), (0, 0), (0, 0)))[:, :S]
        return jnp.concatenate([prev.reshape(B, nb, BLOCK, N_KV_HEADS, HEAD_DIM_2),
                                t.reshape(B, nb, BLOCK, N_KV_HEADS, HEAD_DIM_2)], axis=2)

    kb, vb = kv_blocks(k), kv_blocks(v)
    s = jnp.einsum('bnqhgd,bnkhd->bnhgqk', qb, kb) * (HEAD_DIM_2 ** -0.5)
    qi = jnp.arange(BLOCK)[:, None]
    kj = jnp.arange(2 * BLOCK)[None, :]
    dist = qi + BLOCK - kj
    band = (dist >= 0) & (dist < WINDOW)
    kpos = jnp.arange(nb)[:, None, None] * BLOCK - BLOCK + kj[None]
    mask = band[None] & (kpos >= 0)
    s = jnp.where(mask[None, :, None, None], s, -jnp.inf)
    sink = sinks.astype(jnp.float32).reshape(N_KV_HEADS, Q_PER_KV)[None, None, :, :, None, None]
    m = jnp.maximum(jnp.max(s, axis=-1, keepdims=True), sink)
    pr = jnp.exp(s - m)
    pr = pr / (jnp.sum(pr, axis=-1, keepdims=True) + jnp.exp(sink - m))
    o = jnp.einsum('bnhgqk,bnkhd->bnqhgd', pr, vb)
    return o.reshape(B, S, ATT_Q).astype(q.dtype)

def rwkv7_scan(r, w, k, v, a, b):
    B, S, H, N = r.shape

    def step(state, inp):
        r_t, w_t, k_t, v_t, a_t, b_t = inp
        sa = jnp.einsum('bhvk,bhk->bhv', state, a_t)
        state = (state * w_t[:, :, None, :] + sa[..., None] * b_t[:, :, None, :]
                 + v_t[..., None] * k_t[:, :, None, :])
        return state, jnp.einsum('bhvk,bhk->bhv', state, r_t)

    xs = tuple(jnp.moveaxis(t.astype(jnp.float32), 1, 0) for t in (r, w, k, v, a, b))
    s0 = jnp.zeros((B, H, N, N), jnp.float32)
    _, y = lax.scan(step, s0, xs)
    return jnp.moveaxis(y, 0, 1)

def rwkv7_time_mix(z, mu, w0, w2, a0, a2, g2, k_k, k_a, r_k, gn_w, gn_b):
    B, S = z.shape[0], z.shape[1]
    zs = z + (jnp.pad(z, ((0, 0), (1, 0), (0, 0)))[:, :S] - z) * mu
    r, k, v, wd, ad, gd = _split(zs, (RW_DIM, RW_DIM, RW_DIM, DECAY_RANK, ICLR_RANK, GATE_RANK))
    w = -jax.nn.softplus(-(w0 + jnp.tanh(wd) @ w2)) - 0.5
    decay = jnp.exp(-jnp.exp(w.astype(jnp.float32)))
    iclr = jax.nn.sigmoid(a0 + ad @ a2)
    g = jax.nn.sigmoid(gd) @ g2

    def heads(t):
        return t.astype(jnp.float32).reshape(B, S, RW_HEADS, RW_HEAD)

    kk = heads(k * k_k)
    kk = kk / jnp.maximum(jnp.sqrt(jnp.sum(kk * kk, axis=-1, keepdims=True)), 1e-12)
    k = k * (1.0 + (iclr - 1.0) * k_a)
    rh, kh, vh, ah = heads(r), heads(k), heads(v), heads(iclr)
    y = rwkv7_scan(rh, heads(decay), kh, vh, -kk, kk * ah)
    mean = jnp.mean(y, axis=-1, keepdims=True)
    var = jnp.mean(jnp.square(y - mean), axis=-1, keepdims=True)
    y = ((y - mean) * lax.rsqrt(var + GN_EPS)).reshape(B, S, RW_DIM) * gn_w + gn_b
    bonus = jnp.sum(rh * kh * r_k.astype(jnp.float32), axis=-1, keepdims=True) * vh
    out = (y + bonus.reshape(B, S, RW_DIM)) * g
    return out.astype(z.dtype)

def causal_dwconv(u, w, b):
    C = u.shape[-1]
    y = lax.conv_general_dilated(u, w[:, None, :].astype(u.dtype), window_strides=(1,),
                                 padding=[(CONV_W - 1, 0)],
                                 dimension_numbers=('NWC', 'WIO', 'NWC'),
                                 feature_group_count=C)
    return y + b

def hybrid_layer(x, p_i, positions, norm_mix_pre, w_in, att_sinks, w_o_att, rw_mu, rw_w0,
                 rw_w2, rw_a0, rw_a2, rw_g2, rw_k_k, rw_k_a, rw_r_k, rw_gn_w, rw_gn_b,
                 w_o_rw, w_out, norm_mix_post, norm_ffn_pre, w_up, conv_w, conv_b, w_down,
                 norm_ffn_post, w_ple, w_ple_gate, norm_ple):
    B, S = x.shape[0], x.shape[1]
    h = rmsnorm(x, norm_mix_pre)
    proj = h @ w_in
    q, k, v, rw, gate_a, gate_b = _split(proj, (ATT_Q, ATT_KV, ATT_KV, RW_SHIFT_COLS, D_MODEL, D_MODEL))
    q = rope(q.reshape(B, S, N_Q_HEADS, HEAD_DIM_2), positions)
    k = rope(k.reshape(B, S, N_KV_HEADS, HEAD_DIM_2), positions)
    v = v.reshape(B, S, N_KV_HEADS, HEAD_DIM_2)
    y_att = sliding_window_attention(q, k, v, att_sinks) @ w_o_att
    y_rw = rwkv7_time_mix(rw, rw_mu, rw_w0, rw_w2, rw_a0, rw_a2, rw_g2, rw_k_k, rw_k_a,
                          rw_r_k, rw_gn_w, rw_gn_b) @ w_o_rw
    mixed = jax.nn.sigmoid(gate_a) * y_att + jax.nn.sigmoid(gate_b) * y_rw
    x = x + rmsnorm(mixed @ w_out, norm_mix_post)
    h = rmsnorm(x, norm_ffn_pre)
    u = causal_dwconv(h @ w_up, conv_w, conv_b)
    ua, ub = _split(u, (FFN_DIM, FFN_DIM))
    x = x + rmsnorm((jax.nn.gelu(ua) * ub) @ w_down, norm_ffn_post)
    e = p_i @ w_ple
    gate = jax.nn.sigmoid(x @ w_ple_gate)
    x = x + rmsnorm(gate * e, norm_ple)
    return x

def second_inputs(seed: int = 0) -> dict:
    key = jax.random.key(seed)
    ks = iter(jax.random.split(key, 40))

    def nrm(shape, scale):
        return jax.random.normal(next(ks), shape, jnp.float32) * scale

    def gain(n):
        return 1.0 + nrm((DEPTH, n), 0.05)

    L = DEPTH
    return {
        'x': nrm((BATCH, SEQ, D_MODEL), 1.0),
        'p': nrm((DEPTH, BATCH, SEQ, PLE_DIM), 1.0),
        'positions': jnp.broadcast_to(jnp.arange(SEQ, dtype=jnp.int32)[None], (BATCH, SEQ)),
        'norm_mix_pre': gain(D_MODEL),
        'w_in': nrm((L, D_MODEL, D_IN), D_MODEL ** -0.5),
        'att_sinks': nrm((L, N_Q_HEADS), 0.5),
        'w_o_att': nrm((L, ATT_Q, D_MODEL), ATT_Q ** -0.5),
        'rw_mu': jax.random.uniform(next(ks), (L, RW_SHIFT_COLS), jnp.float32),
        'rw_w0': nrm((L, RW_DIM), 0.5),
        'rw_w2': nrm((L, DECAY_RANK, RW_DIM), DECAY_RANK ** -0.5),
        'rw_a0': nrm((L, RW_DIM), 0.5),
        'rw_a2': nrm((L, ICLR_RANK, RW_DIM), ICLR_RANK ** -0.5),
        'rw_g2': nrm((L, GATE_RANK, RW_DIM), GATE_RANK ** -0.5),
        'rw_k_k': 0.85 + nrm((L, RW_DIM), 0.1),
        'rw_k_a': 1.0 + nrm((L, RW_DIM), 0.1),
        'rw_r_k': nrm((L, RW_HEADS, RW_HEAD), 0.1),
        'rw_gn_w': gain(RW_DIM),
        'rw_gn_b': nrm((L, RW_DIM), 0.01),
        'w_o_rw': nrm((L, RW_DIM, D_MODEL), RW_DIM ** -0.5),
        'w_out': nrm((L, D_MODEL, D_MODEL), D_MODEL ** -0.5),
        'norm_mix_post': gain(D_MODEL),
        'norm_ffn_pre': gain(D_MODEL),
        'w_up': nrm((L, D_MODEL, 2 * FFN_DIM), D_MODEL ** -0.5),
        'conv_w': nrm((L, CONV_W, 2 * FFN_DIM), CONV_W ** -0.5),
        'conv_b': nrm((L, 2 * FFN_DIM), 0.01),
        'w_down': nrm((L, FFN_DIM, D_MODEL), FFN_DIM ** -0.5),
        'norm_ffn_post': gain(D_MODEL),
        'w_ple': nrm((L, PLE_DIM, D_MODEL), PLE_DIM ** -0.5),
        'w_ple_gate': nrm((L, D_MODEL, D_MODEL), D_MODEL ** -0.5),
        'norm_ple': gain(D_MODEL),
    }

def second_block(x, p, positions, norm_mix_pre, w_in, att_sinks, w_o_att, rw_mu, rw_w0, rw_w2,
              rw_a0, rw_a2, rw_g2, rw_k_k, rw_k_a, rw_r_k, rw_gn_w, rw_gn_b, w_o_rw, w_out,
              norm_mix_post, norm_ffn_pre, w_up, conv_w, conv_b, w_down, norm_ffn_post,
              w_ple, w_ple_gate, norm_ple):
    for i in range(DEPTH):
        x = hybrid_layer(x, p[i], positions, norm_mix_pre[i], w_in[i], att_sinks[i], w_o_att[i],
                         rw_mu[i], rw_w0[i], rw_w2[i], rw_a0[i], rw_a2[i], rw_g2[i], rw_k_k[i],
                         rw_k_a[i], rw_r_k[i], rw_gn_w[i], rw_gn_b[i], w_o_rw[i], w_out[i],
                         norm_mix_post[i], norm_ffn_pre[i], w_up[i], conv_w[i], conv_b[i],
                         w_down[i], norm_ffn_post[i], w_ple[i], w_ple_gate[i], norm_ple[i])
    return x


def setup_inputs(seed=0):
    out = dict(first_inputs(seed))
    for name, value in second_inputs(seed + 1).items():
        if name != "x":
            out[name + "_2"] = value
    return out


def reference(
    x, c, w_in, w_out, ret_norm_w, hgrn_norm_w, hgrn_lb_logits, norm1_w, norm2_w, ada_w, ada_b,
    w_gate, w_val, conv_w, conv_b, w_down, final_norm_w, p_2, positions_2, norm_mix_pre_2,
    w_in_2, att_sinks_2, w_o_att_2, rw_mu_2, rw_w0_2, rw_w2_2, rw_a0_2, rw_a2_2, rw_g2_2,
    rw_k_k_2, rw_k_a_2, rw_r_k_2, rw_gn_w_2, rw_gn_b_2, w_o_rw_2, w_out_2, norm_mix_post_2,
    norm_ffn_pre_2, w_up_2, conv_w_2, conv_b_2, w_down_2, norm_ffn_post_2, w_ple_2,
    w_ple_gate_2, norm_ple_2,
):
    x = first_block(
        x, c, w_in, w_out, ret_norm_w, hgrn_norm_w, hgrn_lb_logits, norm1_w, norm2_w, ada_w,
        ada_b, w_gate, w_val, conv_w, conv_b, w_down, final_norm_w,
    )
    return second_block(
        x, p_2, positions_2, norm_mix_pre_2, w_in_2, att_sinks_2, w_o_att_2, rw_mu_2, rw_w0_2,
        rw_w2_2, rw_a0_2, rw_a2_2, rw_g2_2, rw_k_k_2, rw_k_a_2, rw_r_k_2, rw_gn_w_2, rw_gn_b_2,
        w_o_rw_2, w_out_2, norm_mix_post_2, norm_ffn_pre_2, w_up_2, conv_w_2, conv_b_2,
        w_down_2, norm_ffn_post_2, w_ple_2, w_ple_gate_2, norm_ple_2,
    )


_drawn_inputs = setup_inputs


def setup_inputs(seed=0):
    import zlib

    import numpy as np

    out = dict(_drawn_inputs(seed))
    spreads = {}
    factors = {'ret_norm_w': 6.259,
     'hgrn_norm_w': 5.295,
     'hgrn_lb_logits': 8.0,
     'norm2_w': 2.92,
     'conv_b': 8.0,
     'att_sinks_2': 4.739,
     'rw_gn_b_2': 4.947,
     'conv_b_2': 4.929}
    for name, (base, spread) in spreads.items():
        noise = np.random.default_rng([zlib.crc32(name.encode()), seed]).standard_normal(out[name].shape)
        drawn = base * np.exp(spread * noise) if base else spread * noise
        out[name] = __import__('jax').numpy.asarray(drawn.astype(out[name].dtype))
    for name, factor in factors.items():
        out[name] = (out[name] * factor).astype(out[name].dtype)
    return out
```

```python
from contextlib import ExitStack

import numpy as np
import concourse.bass as bass
from concourse import mybir

F32 = mybir.dt.float32
F32R = mybir.dt.float32r
I32 = mybir.dt.int32
ALU = mybir.AluOpType
ACT = mybir.ActivationFunctionType
AX = mybir.AxisListType

P = 128
D = 1024
S = 512
KD = D // P
DEPTH = 2
EPS = 1e-6
GN_EPS = 64e-5
FF = 2816
KF = FF // P
SPLIT = 2


class Flow:

    def __init__(self, sem, name, depth, readers=1):
        self.full = sem(f"{name}_full")
        self.free = [sem(f"{name}_free{r}") for r in range(readers)]
        self.depth = depth
        self.claimed = self.made = 0
        self.got = [0] * readers

    def claim(self, eng):
        n = self.claimed
        self.claimed += 1
        if n >= self.depth:
            for f in self.free:
                eng.wait_ge(f, n - self.depth + 1)
        return n % self.depth

    def put(self):
        self.made += 1
        return self.full, self.made

    def get(self, eng, r=0):
        n = self.got[r]
        self.got[r] += 1
        eng.wait_ge(self.full, n + 1)
        return n % self.depth

    def drop(self, r=0):
        return self.free[r], self.got[r]


class Steps:

    def __init__(self, eng, own):
        self.eng, self.own, self.count, self.last = eng, own, 0, None

    def do(self, ins, signal=None):
        if signal is None:
            self.count += 1
            signal = (self.own, self.count)
        ins.then_inc(signal[0], 1)
        self.last = signal
        return signal

    def settle(self):
        if self.last is not None:
            self.eng.wait_ge(*self.last)


class Scope:

    def __init__(self, nc, ctx, tag):
        self.nc, self.ctx, self.tag, self.sems = nc, ctx, tag, []

    def sb(self, name, shape, dt=F32):
        return self.ctx.enter_context(self.nc.sbuf_tensor(f"{self.tag}_{name}", shape, dt))

    def ps(self, name, shape):
        return self.ctx.enter_context(self.nc.psum_tensor(f"{self.tag}_{name}", shape, F32))

    def sem(self, name):
        s = self.ctx.enter_context(self.nc.semaphore(f"{self.tag}_{name}"))
        self.sems.append(s)
        return s

    def flow(self, name, depth, readers=1):
        return Flow(self.sem, name, depth, readers)

    def clear(self):
        nc = self.nc
        engines = (nc.gpsimd, nc.vector, nc.scalar, nc.tensor, nc.sync)
        for i, s in enumerate(self.sems):
            engines[i % 5].sem_clear(s)
        self.nc.all_engine_barrier()


class Weights:

    def __init__(self, sc, units, raw=4):
        self.units, self.ring = units, raw
        self.raw = sc.sb("w_raw", [P, raw, D])
        self.hi = sc.sb("w_hi", [P, SPLIT, D], F32R)
        self.lo = sc.sb("w_lo", [P, SPLIT, D], F32R)
        self.loaded = [sc.sem(f"w_loaded{i}") for i in range(raw)]
        self.hi_made = sc.sem("w_hi_made")
        self.lo_made = sc.sem("w_lo_made")
        self.used = sc.sem("w_used")
        self.hi_at = 0
        self.taken = 0

    def load(self, sp, n):
        src, width = self.units[n]
        if n >= self.ring:
            sp.wait_ge(self.lo_made, n - self.ring + 1)
        sp.dma_start(self.raw[:, n % self.ring, 0:width], src).then_inc(self.loaded[n % self.ring], 16)

    def high(self, st, upto):
        while self.hi_at <= min(upto, len(self.units) - 1):
            n, width = self.hi_at, self.units[self.hi_at][1]
            self.hi_at += 1
            st.eng.wait_ge(self.loaded[n % self.ring], 16 * (n // self.ring + 1))
            if n >= SPLIT:
                st.eng.wait_ge(self.used, n - SPLIT + 1)
            st.do(st.eng.activation(self.hi[:, n % SPLIT, 0:width], self.raw[:, n % self.ring, 0:width], ACT.Copy),
                  (self.hi_made, n + 1))

    def low(self, st, n):
        width = self.units[n][1]
        st.eng.wait_ge(self.hi_made, n + 1)
        st.do(st.eng.tensor_tensor(self.lo[:, n % SPLIT, 0:width], self.raw[:, n % self.ring, 0:width],
                                   self.hi[:, n % SPLIT, 0:width].bitcast(F32), ALU.subtract),
              (self.lo_made, n + 1))

    def take(self, pe):
        n = self.taken
        self.taken += 1
        pe.wait_ge(self.lo_made, n + 1)
        return n % SPLIT

    def blocks(self, pe, out, hh, hl, k0=0, first=True, last=True, ready=None):
        s, ks = self.take(pe), self.units[self.taken - 1][1] // P
        for k in range(ks):
            a = slice(k * P, (k + 1) * P)
            if ready is not None:
                pe.wait_ge(ready, k0 + k + 1)
            pe.matmul(out, self.hi[:, s, a], hh[:, k0 + k, :], start=first and k == 0, stop=False)
            pe.matmul(out, self.hi[:, s, a], hl[:, k0 + k, :], start=False, stop=False)
            mm = pe.matmul(out, self.lo[:, s, a], hh[:, k0 + k, :], start=False, stop=last and k == ks - 1)
            if k == ks - 1:
                mm.then_inc(self.used, 1)
            yield k

    def project(self, pe, out, hh, hl, k0=0, first=True, last=True, between=None, ready=None):
        for k in self.blocks(pe, out, hh, hl, k0, first, last, ready):
            if between is not None:
                between(k)

    def project_tokens(self, pe, outs, hh, hl, u, cols, ready=None):
        s = self.take(pe)
        nk = D // cols
        for j in range(nk):
            k, b = u * nk + j, slice(j * cols, (j + 1) * cols)
            if ready is not None:
                pe.wait_ge(ready, k + 1)
            for t, out in enumerate(outs):
                a = slice(t * P, (t + 1) * P)
                pe.matmul(out, hh[:, k, a], self.hi[:, s, b], start=k == 0, stop=False)
                pe.matmul(out, hh[:, k, a], self.lo[:, s, b], start=False, stop=False)
                mm = pe.matmul(out, hl[:, k, a], self.hi[:, s, b], start=False, stop=k == KD - 1)
        mm.then_inc(self.used, 1)


class Norm:

    def __init__(self, sc, h_hi, h_lo, sq, xn, h, acc, rstd):
        self.sq, self.xn, self.h, self.acc, self.rstd = sq, xn, h, acc, rstd
        self.hh, self.hl = h_hi, h_lo
        self.f_sq = sc.flow("norm_sq", 2)
        self.f_sum = sc.flow("norm_sum", 1)
        self.f_acc = sc.flow("norm_acc", 1)
        self.f_rstd = sc.flow("norm_rstd", 1)
        self.f_xn = sc.flow("norm_xn", 2)
        self.f_h = sc.flow("norm_h", 2)
        self.f_hi = sc.flow("norm_hi", KD)
        self.f_lo = sc.flow("norm_lo", KD)

    def act_sums(self, st, x, bank, eps_col, ws):
        for k in range(KD):
            b = self.f_sq.claim(st.eng)
            st.do(st.eng.activation(self.sq[:, b, :], x[:, k, :], ACT.Square), self.f_sq.put())
        ws.high(st, 1)
        st.do(st.eng.activation(self.rstd[:, 0:1], eps_col, ACT.Ln))
        st.settle()
        self.f_sum.get(st.eng)
        st.do(st.eng.activation(self.rstd[:, :], bank[:, :], ACT.Ln, scale=1.0 / D, bias=eps_col), self.f_sum.drop())
        st.settle()
        st.do(st.eng.activation(self.rstd[:, :], self.rstd[:, :], ACT.Exp, scale=-0.5), self.f_rstd.put())

    def act_affine(self, st, scale, shift):
        for k in range(KD):
            b = self.f_xn.get(st.eng)
            self.f_h.claim(st.eng)
            bias = shift[:, k:k + 1] if shift is not None else 0.0
            st.do(st.eng.activation(self.h[:, b, :], self.xn[:, b, :], ACT.Identity,
                                    scale=scale[:, k:k + 1], bias=bias), self.f_h.put())

    def dve_sums(self, st):
        for k in range(KD):
            b = self.f_sq.get(st.eng)
            if k == 0:
                st.settle()
                st.do(st.eng.tensor_copy(self.acc[:, :], self.sq[:, b, :]), self.f_sq.drop())
            elif k < KD - 1:
                st.settle()
                st.do(st.eng.tensor_tensor(self.acc[:, :], self.acc[:, :], self.sq[:, b, :], ALU.add), self.f_sq.drop())
            else:
                st.settle()
                st.do(st.eng.tensor_tensor(self.acc[:, :], self.acc[:, :], self.sq[:, b, :], ALU.add), self.f_acc.put())

    def dve_normalise(self, st, x):
        self.f_rstd.get(st.eng)
        for k in range(KD + 1):
            if k < KD:
                if k >= 2:
                    st.eng.wait_ge(self.f_h.full, k - 1)
                b = k % 2
                st.do(st.eng.tensor_tensor(self.xn[:, b, :], x[:, k, :], self.rstd[:, :], ALU.mult), self.f_xn.put())
            if k >= 1:
                b = self.f_h.get(st.eng)
                st.do(st.eng.tensor_copy(self.hh[:, k - 1, :], self.h[:, b, :]), self.f_hi.put())

    def pool(self, st, ws):
        ws.low(st, 0)
        ws.low(st, 1)
        for k in range(KD):
            st.eng.wait_ge(self.f_hi.full, k + 1)
            st.do(st.eng.tensor_tensor(self.hl[:, k, :], self.h[:, k % 2, :], self.hh[:, k, :].bitcast(F32),
                                       ALU.subtract), (self.f_h.free[0], k + 1))

    def pe(self, eng, bank, ones):
        self.f_acc.get(eng)
        eng.matmul(bank[:, :], ones[:, :], self.acc[:, :], start=True, stop=True).then_inc(self.f_sum.put()[0], 1)

    @property
    def ready(self):
        return self.f_h.free[0]


class Ada:

    def __init__(self, sc, bank, c_act, ones, units, slots=2):
        self.SLOTS = slots
        self.units, self.bank, self.c_act, self.ones = units, bank, c_act, ones
        self.raw = sc.sb("ada_raw", [P, self.SLOTS, D])
        self.rows = sc.sb("ada_rows", [P, 2, P])
        self.loaded = [sc.sem(f"ada_loaded{i}") for i in range(self.SLOTS)]
        self.scaled, self.summed, self.used = sc.sem("ada_scaled"), sc.sem("ada_summed"), sc.sem("ada_used")
        self.at = 0

    def load(self, sp, n):
        if n >= self.SLOTS:
            sp.wait_ge(self.summed, n - self.SLOTS + 1)
        sp.dma_start(self.raw[:, n % self.SLOTS, :], self.units[n]).then_inc(self.loaded[n % self.SLOTS], 16)

    def scale(self, st, n):
        s = n % self.SLOTS
        st.eng.wait_ge(self.loaded[s], 16 * (n // self.SLOTS + 1))
        w = self.raw[:, s, :].rearrange("p (k m) -> p k m", k=KD)
        c = self.c_act[:, :].unsqueeze(2).broadcast_to([P, KD, P])
        st.do(st.eng.tensor_tensor(w, w, c, ALU.mult), (self.scaled, n + 1))

    def add(self, st, n):
        st.eng.wait_ge(self.scaled, n + 1)
        if n >= 2:
            st.eng.wait_ge(self.used, n - 1)
        w = self.raw[:, n % self.SLOTS, :].rearrange("p (k m) -> p m k", k=KD)
        st.do(st.eng.tensor_reduce(self.rows[:, n % 2, :], w, AX.X, ALU.add), (self.summed, n + 1))

    def product(self, pe):
        n = self.at
        self.at += 1
        pe.wait_ge(self.summed, n + 1)
        mm = pe.matmul(self.bank[:, n:n + 1], self.rows[:, n % 2, :], self.ones[:, 0:1], start=True, stop=True)
        mm.then_inc(self.used, 1)


A_COLS = {"norm1": 8, "norm2": 8, "ret_w": 4, "hgrn_w": 4, "lb0": 4, "lb1": 4, "lsel": 1, "ada_b": 32, "ada_b_next": 16,
          "conv0": KF, "conv1": KF, "conv2": KF, "conv_b": KF}
RW = 1024
B_COLS = {"norm_mix_pre": 8, "mu_r": 8, "mu_k": 8, "mu_v": 8, "mu_wa": 1, "mu_g": 2, "w0": 8, "a0": 8, "k_k": 8,
          "k_a": 8, "r_k": 8, "gn_w": 8, "gn_b": 8, "norm_mix_post": 8, "norm_ffn_pre": 8, "conv0": 2 * KF,
          "conv1": 2 * KF, "conv2": 2 * KF, "conv_b": 2 * KF, "norm_ffn_post": 8, "norm_ple": 8}


def offsets(cols):
    at, out = 0, {}
    for name, n in cols.items():
        out[name] = (at, at + n)
        at += n
    return out, at


A_AT, A_N = offsets(A_COLS)
B_AT, B_N = offsets(B_COLS)
HEADS = 4
LEVELS = 7


def prologue(nc, io, keep):
    with ExitStack() as ctx:
        sc = Scope(nc, ctx, "pro")
        bank = sc.ps("bank", [P, 512])
        ada = Ada(sc, bank, keep["c_act"], keep["ones"], [io["ada_first"][n] for n in range(16)], slots=8)
        par = sc.sb("par", [P, 16])
        e = sc.sb("e", [P, KD])
        in_ = sc.sem("in")
        c_made, sig, dve_own, pool_own = sc.sem("c_made"), sc.sem("sig"), sc.sem("dve_own"), sc.sem("pool_own")
        with nc.Block() as block:
            @block.sync
            def _(sp):
                sp.dma_start(keep["c_raw"][:, :], io["c"]).then_inc(in_, 16)
                sp.dma_start(par[:, :], io["ada_b_first"]).then_inc(in_, 16)
                sp.dma_start(keep["ones"][:, :], io["ones"]).then_inc(in_, 16)
                sp.dma_start(keep["eye"][:, :], io["eye"]).then_inc(in_, 16)
                for n in range(16):
                    ada.load(sp, n)
                sp.dma_start(keep["x"][:, :, :], io["x"]).then_inc(in_, 16)
                sp.wait_ge(in_, 80)

            @block.scalar
            def _(act):
                act.wait_ge(in_, 64)
                act.activation(e[:, :], keep["c_raw"][:, :], ACT.Exp, scale=-1.0).then_inc(sig, 1)

            @block.vector
            def _(dve):
                st = Steps(dve, dve_own)
                for i, value in enumerate((EPS, 10.0 * float(np.log(2.0)), GN_EPS, 0.5)):
                    st.do(dve.memset(keep["eps"][:, i:i + 1], value))
                dve.wait_ge(in_, 64)
                dve.wait_ge(sig, 1)
                st.do(dve.tensor_scalar(e[:, :], e[:, :], 1.0, None, ALU.add))
                st.settle()
                st.do(dve.reciprocal(e[:, :], e[:, :]))
                st.settle()
                st.do(dve.tensor_tensor(keep["c_act"][:, :], keep["c_raw"][:, :], e[:, :], ALU.mult), (c_made, 1))
                for n in range(16):
                    ada.add(st, n)
                dve.wait_ge(ada.used, 16)
                st.do(dve.tensor_tensor(keep["mod_pre"][:, :], bank[:, 0:16], par[:, :], ALU.add))

            @block.gpsimd
            def _(pool):
                st = Steps(pool, pool_own)
                pool.wait_ge(c_made, 1)
                for n in range(16):
                    ada.scale(st, n)

            @block.tensor
            def _(pe):
                for _ in range(16):
                    ada.product(pe)
        sc.clear()


def mixer_a(nc, io, keep, l):
    with ExitStack() as ctx:
        sc = Scope(nc, ctx, "ma")
        x = keep["x"]
        banks = [sc.ps(f"bank{i}", [P, 512]) for i in range(8)]
        par = sc.sb("par", [P, A_N])
        hh, hl = sc.sb("h_hi", [P, KD, S], F32R), sc.sb("h_lo", [P, KD, S], F32R)
        mh, ml = sc.sb("m_hi", [P, KD, S], F32R), sc.sb("m_lo", [P, KD, S], F32R)
        units = [(io["a_wv"][l, g, u], D) for g in range(2) for u in range(4)]
        units += [(io["a_wh"][l, g, n], D) for g in range(2) for n in range(12)]
        units += [(io["a_wo"][l, n], D) for n in range(KD)]
        first_out = 8 + 24
        ws = Weights(sc, units)
        ada = Ada(sc, banks[7], keep["c_act"], keep["ones"], [io["ada"][l, n] for n in range(32)])
        cos, sin = sc.sb("cos", [P, S]), sc.sb("sin", [P, S])
        decay = sc.sb("decay", [P, HEADS, S])
        masks = sc.sb("masks", [P, LEVELS, P], I32)
        reset = sc.sb("reset", [P, S])
        scale1 = sc.sb("scale1", [P, KD])
        raw, sw = sc.sb("raw", [P, 2, S]), sc.sb("sw", [P, 2, S])
        rot = sc.sb("rot", [P, 2, 2, S])
        gate = sc.sb("gate", [P, 2, S])
        v_tok = sc.sb("v_tok", [P, 2, 4, S])
        kept = sc.sb("kept", [P, 1280])
        osq, orstd, merged = sc.sb("osq", [P, S]), sc.sb("orstd", [P, S]), sc.sb("merged", [P, S])
        sg = sc.sb("sg", [P, S])
        rs = sc.sb("rs", [P, S])
        hset = sc.sb("hset", [P, 3, S])
        omlb = sc.sb("omlb", [P, HEADS])
        lbt = sc.sb("lbt", [P, HEADS])
        lbw = sc.sb("lbw", [P, 2, HEADS])
        eb = sc.sb("eb", [P, 2])
        cum = [hset[:, 0, :], rot[:, 0, 1, :]]
        kin = [hset[:, 1, :], rot[:, 1, 0, :]]
        qin = [hset[:, 2, :], rot[:, 1, 1, :]]
        ez, ln_a, ln_b = rot[:, 0, 0, :], cos, sin
        diff, qk = raw, sw
        kx, qx = decay[:, 0, :], decay[:, 1, :]
        ek, eq = decay[:, 2, 0:384], decay[:, 3, 0:384]
        near, far = kept[:, 0:512], kept[:, 512:1280]
        norm = Norm(sc, hh, hl, raw, sw, gate, osq, orstd)

        par_in, const_in = sc.sem("par_in"), sc.sem("const_in")
        par_made = sc.sem("par_made")
        v_used = sc.sem("v_used")
        p_free = sc.sem("p_free")
        sw_in = [sc.sem("sw_in0"), sc.sem("sw_in1")]
        rot_made, sg_made, sg_used = sc.sem("rot_made"), sc.sem("sg_made"), sc.sem("sg_used")
        lbd_made, lbe_made, merged_made = sc.sem("lbd_made"), sc.sem("lbe_made"), sc.sem("merged_made")
        s_made, m_made = sc.sem("s_made"), sc.sem("m_made")
        o_made, o_free = sc.sem("o_made"), sc.sem("o_free")
        sq_made, sum_made, six_free, r_made = sc.sem("sq_made"), sc.sem("sum_made"), sc.sem("six_free"), sc.sem("r_made")
        mm_made = sc.sem("mm_made")
        ez_made, ezc_made, z_made = sc.sem("ez_made"), sc.sem("ezc_made"), sc.sem("z_made")
        b_made, kin_made = sc.sem("b_made"), sc.sem("kin_made")
        d_made, e_made, qk_made = sc.sem("d_made"), sc.sem("e_made"), sc.sem("qk_made")
        l_made, l_free = sc.sem("l_made"), sc.sem("l_free")
        ex_made, fx_made, far4_made, far6_made, far_kept = (sc.sem("ex_made"), sc.sem("fx_made"), sc.sem("far4_made"),
                                                            sc.sem("far6_made"), sc.sem("far_kept"))
        y_made, y_free, mod_made = sc.sem("y_made"), sc.sem("y_free"), sc.sem("mod_made")
        own_a, own_v, own_p = sc.sem("act_own"), sc.sem("dve_own"), sc.sem("pool_own")

        def ada_at(k):
            return k * 3 // 4

        def cols(name):
            return par[:, A_AT[name][0]:A_AT[name][1]]

        def col(name, i):
            return par[:, A_AT[name][0] + i:A_AT[name][0] + i + 1]

        with nc.Block() as block:
            @block.sync
            def _(sp):
                sp.dma_start(par[:, :], io["a_par"][l]).then_inc(par_in, 16)
                for n in range(len(units)):
                    ws.load(sp, n)
                    if n == 3:
                        sp.dma_start(cos[:, :], io["a_cos"]).then_inc(const_in, 16)
                        sp.dma_start(sin[:, :], io["a_sin"]).then_inc(const_in, 16)
                        sp.dma_start(decay[:, :, :], io["a_decay"]).then_inc(const_in, 16)
                        sp.dma_start(masks[:, :, :], io["a_masks"]).then_inc(const_in, 16)
                        sp.dma_start(reset[:, :], io["a_reset"]).then_inc(const_in, 16)
                    for k in range(32):
                        if 8 + ada_at(k) + 2 == n:
                            ada.load(sp, k)

            @block.gpsimd
            def _(pool):
                st = Steps(pool, own_p)
                norm.pool(st, ws)
                for n in range(2, len(units)):
                    ws.low(st, n)
                    for k in range(32):
                        if 8 + ada_at(k) == n:
                            ada.scale(st, k)

            @block.scalar
            def _(act):
                st = Steps(act, own_a)

                def silu_parts(i, dst):
                    st.settle()
                    st.do(act.activation(dst, banks[i % 2][:, :], ACT.Copy))
                    if sg_count[0]:
                        act.wait_ge(sg_used, sg_count[0])
                    st.settle()
                    st.do(act.activation(sg[:, :], banks[i % 2][:, :], ACT.Tanh, scale=0.5), (p_free, i + 1))
                    st.settle()
                    st.do(act.activation(sg[:, :], sg[:, :], ACT.Identity, scale=0.5, bias=keep["eps"][:, 3:4]),
                          (sg_made, sg_count[0] + 1))
                    sg_count[0] += 1

                sg_count = [0]

                def exps(h, levels):
                    for li in levels:
                        g = 7 * h + li - 1
                        act.wait_ge(d_made, g + 1)
                        st.do(act.activation(diff[:, g % 2, :], diff[:, g % 2, :], ACT.Exp), (e_made, g + 1))

                def far_exps(h):
                    b = cum[h % 2]
                    act.wait_ge(b_made, h + 1)
                    if h:
                        act.wait_ge(fx_made, h)
                    for c in range(3):
                        st.settle()
                        st.do(act.activation(ek[:, c * P:(c + 1) * P], b[:, c * P:(c + 1) * P], ACT.Exp, scale=-1.0,
                                             bias=b[:, c * P + P - 1:c * P + P]))
                    st.settle()
                    st.do(act.activation(eq[:, :], b[:, P:S], ACT.Exp))
                    st.settle()
                    st.do(act.activation(eb[:, :], b[:, 2 * P - 1:3 * P:P], ACT.Exp), (ex_made, h + 1))

                def far_keep(h):
                    act.wait_ge(far4_made, h + 1)
                    act.wait_ge(o_made, HEADS + h)
                    st.settle()
                    st.do(act.activation(far[:, 0:512], banks[4][:, :], ACT.Copy))
                    act.wait_ge(far6_made, h + 1)
                    st.settle()
                    st.do(act.activation(far[:, 512:768], banks[6][:, 0:256], ACT.Copy), (six_free, 5 + 2 * h))

                def squares(H):
                    act.wait_ge(o_made, H + 1)
                    st.settle()
                    st.do(act.activation(osq[:, :], banks[5][:, :], ACT.Square), (sq_made, H + 1))

                def head_rstd(H):
                    act.wait_ge(sum_made, H + 1)
                    if H:
                        act.wait_ge(o_free, H)
                    st.settle()
                    st.do(act.activation(orstd[:, :], banks[6][:, :], ACT.Ln, scale=1.0 / P, bias=keep["eps"][:, 0:1]),
                          (six_free, H + 1 if H < HEADS else 2 * H - 2))
                    st.settle()
                    st.do(act.activation(orstd[:, :], orstd[:, :], ACT.Exp, scale=-0.5), (r_made, H + 1))

                norm.act_sums(st, x, banks[6], keep["eps"][:, 0:1], ws)
                act.wait_ge(par_made, 1)
                norm.act_affine(st, scale1, keep["mod_pre"][:, 0:KD])
                act.wait_ge(lbd_made, 1)
                st.do(act.activation(lbw[:, :, :], lbw[:, :, :], ACT.Exp), (lbe_made, 1))
                for n in range(8):
                    ws.high(st, n + 1)
                    if n % 4 == 3:
                        act.wait_ge(ws.used, n + 1)
                        for t in range(4):
                            st.settle()
                            st.do(act.activation(v_tok[:, n // 4, t, :], banks[2 + t][:, :], ACT.Copy),
                                  (v_used, 4 * (n // 4) + t + 1))
                for G in range(9):
                    J = G - 1
                    for u in range(3):
                        i = 3 * G + u
                        if G < 8 or u == 0:
                            ws.high(st, 8 + i + 1)
                        if 0 <= J < 4:
                            if u == 1:
                                squares(J)
                            if u == 2:
                                head_rstd(J)
                        if J >= 4:
                            h = J - 4
                            if u == 0:
                                exps(h, [3, 4])
                                far_exps(h)
                                exps(h, [5])
                            if u == 1:
                                exps(h, [6, 7])
                            if u == 2:
                                far_keep(h)
                                squares(J)
                                head_rstd(J)
                        if G == 8:
                            continue
                        act.wait_ge(ws.used, 8 + i + 1)
                        if u == 2:
                            if G >= 2:
                                act.wait_ge(mm_made, G - 1)
                            silu_parts(i, gate[:, G % 2, :])
                        elif G < 4:
                            j = 2 * G + u
                            if j >= 2:
                                act.wait_ge(rot_made, j - 1)
                            st.do(act.activation(raw[:, u, :], banks[i % 2][:, :], ACT.Copy), (p_free, i + 1))
                            st.settle()
                            act.dma_start(sw[0:64, u, :], raw[64:128, u, :]).then_inc(sw_in[u], 16)
                            act.dma_start(sw[64:128, u, :], raw[0:64, u, :]).then_inc(sw_in[u], 16)
                        elif u == 0:
                            h = G - 4
                            if h:
                                act.wait_ge(kin_made, h)
                            st.settle()
                            st.do(act.activation(ez, banks[i % 2][:, :], ACT.Exp, scale=-1.0), (p_free, i + 1))
                            if h == 0:
                                act.wait_ge(par_made, 2)
                            act.wait_ge(ezc_made, h + 1)
                            st.do(act.activation(ln_a[:, :], ez, ACT.Ln, scale=lbt[:, h:h + 1], bias=1.0))
                            st.settle()
                            st.do(act.activation(ln_b[:, :], ez, ACT.Ln, bias=1.0))
                            st.settle()
                            st.do(act.activation(rs[:, :], ln_b[:, :], ACT.Exp, scale=-1.0), (z_made, h + 1))
                        else:
                            silu_parts(i, qin[(G - 4) % 2])
                            exps(G - 4, [1, 2])
                ws.high(st, len(units) - 1)

            @block.tensor
            def _(pe):
                eye, ones = keep["eye"], keep["ones"]
                six = [0]

                def six_claim():
                    if six[0]:
                        pe.wait_ge(six_free, six[0])
                    six[0] += 1

                norm.pe(pe, banks[6], ones)
                for g in range(2):
                    if g:
                        pe.wait_ge(v_used, 4)
                    for u in range(4):
                        ws.project_tokens(pe, [banks[2 + t][:, :] for t in range(4)], hh, hl, u, S,
                                          norm.ready if g == 0 else None)
                pe.wait_ge(v_used, 8)

                def scores(h):
                    q, k = rot[:, h % 2, 0, :], rot[:, h % 2, 1, :]
                    pe.wait_ge(rot_made, 2 * h + 2)
                    for j in range(4):
                        if h and j < 3:
                            pe.wait_ge(m_made, 3 * (h - 1) + j + 1)
                        out = banks[2 + j][:, 0:S - j * P] if j < 3 else banks[4][:, 256:384]
                        mm = pe.matmul(out, k[:, j * P:(j + 1) * P], q[:, j * P:S], start=True, stop=True)
                        if j != 2:
                            mm.then_inc(s_made, 1)

                def values(h):
                    at = [0, 512, 896, 1152]
                    if h:
                        pe.wait_ge(o_free, h)
                    for j in range(4):
                        pe.wait_ge(m_made, 3 * h + min(j, 2) + 1)
                        mm = pe.matmul(banks[5][:, j * P:S], v_tok[:, 0, j, h * P:(h + 1) * P],
                                       kept[:, at[j]:at[j] + S - j * P], start=j == 0, stop=j == 3)
                    mm.then_inc(o_made, 1)

                def head_sum(H):
                    pe.wait_ge(sq_made, H + 1)
                    six_claim()
                    pe.matmul(banks[6][:, :], ones[:, :], osq[:, :], start=True, stop=True).then_inc(sum_made, 1)

                def level(h, li):
                    f = 8 * h + li
                    if f >= 2:
                        pe.wait_ge(l_free, f - 1)
                    else:
                        pe.wait_ge(m_made, 12)
                    if li == 0:
                        pe.wait_ge(kin_made, h + 1)
                        pe.wait_ge(sg_used, HEADS + 2 * h + 1)
                        a, b = kin[h % 2], qin[h % 2]
                    else:
                        g = 7 * h + li - 1
                        pe.wait_ge(qk_made, g + 1)
                        a = b = qk[:, g % 2, :]
                    for c in range(4):
                        t = slice(c * P, (c + 1) * P)
                        mm = pe.matmul(banks[2 + f % 2][:, t], a[:, t], b[:, t], start=True, stop=True)
                    mm.then_inc(l_made, 1)

                def far_scores(h):
                    pe.wait_ge(fx_made, h + 1)
                    six_claim()
                    pe.matmul(banks[4][:, 0:128], kx[:, 0:128], qx[:, 0:128], start=True, stop=True)
                    pe.matmul(banks[4][:, 128:256], kx[:, 256:384], qx[:, 384:512], start=True, stop=True)
                    pe.matmul(banks[4][:, 256:512], kx[:, 128:256], qx[:, 128:384], start=True, stop=True)\
                        .then_inc(far4_made, 1)
                    pe.matmul(banks[6][:, 0:256], kx[:, 384:512], qx[:, 128:384], start=True, stop=True)\
                        .then_inc(far6_made, 1)

                def far_values(h):
                    H, v = HEADS + h, lambda j: v_tok[:, 1, j, h * P:(h + 1) * P]
                    out = banks[5]
                    pe.wait_ge(o_free, H)
                    pe.wait_ge(l_free, 8 * h + 8)
                    for j in range(4):
                        t = slice(j * P, (j + 1) * P)
                        pe.matmul(out[:, t], v(j), near[:, t], start=j == 0, stop=False)
                    pe.wait_ge(six_free, 5 + 2 * h)
                    pe.matmul(out[:, 128:256], v(0), far[:, 0:128], start=False, stop=False)
                    pe.matmul(out[:, 384:512], v(2), far[:, 128:256], start=False, stop=False)
                    pe.matmul(out[:, 256:512], v(1), far[:, 256:512], start=False, stop=False)
                    pe.matmul(out[:, 256:512], v(0), far[:, 512:768], start=False, stop=True).then_inc(o_made, 1)

                def job(J, point):
                    if 0 <= J < 4:
                        if point == 1:
                            scores(J)
                        if point == 5:
                            values(J)
                        if point == 8:
                            head_sum(J)
                    elif J >= 4:
                        if point < 8:
                            level(J - 4, point)
                        if point == 8:
                            far_scores(J - 4)
                        if point == 9:
                            far_values(J - 4)
                        if point == 11:
                            head_sum(J)

                for G in range(8):
                    for u in range(3):
                        i = 3 * G + u
                        if i >= 2:
                            pe.wait_ge(p_free, i - 1)

                        def between(k):
                            if k % 2:
                                job(G - 1, 4 * u + k // 2)
                        ws.project(pe, banks[i % 2][:, :], hh, hl, between=between)
                        for k in range(32):
                            if ada_at(k) == i:
                                ada.product(pe)
                pe.wait_ge(p_free, 24)
                pe.wait_ge(merged_made, 7)
                early = [ws.blocks(pe, banks[n][:, :], mh, ml) for n in range(2)]
                for point in range(14):
                    next(early[point // 7])
                    if point < 12:
                        job(7, point)
                pe.wait_ge(merged_made, 8)
                for rest in early:
                    for _ in rest:
                        pass
                for n in range(2, KD):
                    pe.wait_ge(y_free, n - 1)
                    ws.project(pe, banks[n % 2][:, :], mh, ml)

            def lower_bounds(st):
                dve = st.eng
                for i in range(2):
                    st.settle()
                    st.do(dve.tensor_copy(lbw[:, i, :], cols(f"lb{i}")))
                st.settle()
                st.do(dve.tensor_tensor(lbt[:, :], lbw[:, 0, :], lbw[:, 1, :], ALU.max))
                st.settle()
                st.do(dve.tensor_tensor(lbw[:, 0, :], lbw[:, 0, :], lbt[:, :], ALU.subtract))
                st.settle()
                st.do(dve.tensor_tensor(lbw[:, 1, :], lbw[:, 1, :], lbt[:, :], ALU.subtract), (lbd_made, 1))
                dve.wait_ge(lbe_made, 1)
                st.do(dve.tensor_tensor(lbt[:, :], lbw[:, 0, :], lbw[:, 1, :], ALU.add))
                st.settle()
                st.do(dve.reciprocal(lbt[:, :], lbt[:, :]))
                for i in range(2):
                    st.settle()
                    st.do(dve.tensor_tensor(lbw[:, i, :], lbw[:, i, :], lbt[:, :], ALU.mult))
                st.settle()
                st.do(dve.tensor_tensor(lbt[:, :], lbw[:, 0, :], lbw[:, 1, :], ALU.add))
                st.settle()
                st.do(dve.tensor_tensor(lbt[:, :], lbt[:, :], lbw[:, 0, :], ALU.subtract))
                st.settle()
                st.do(dve.tensor_scalar(lbt[:, :], lbt[:, :], col("lsel", 0), None, ALU.mult))

            def mask_scores(st, h):
                dve = st.eng
                if h:
                    dve.wait_ge(o_made, h)
                at = [0, 512, 896, 1152]
                for j in range(4):
                    if j != 3:
                        dve.wait_ge(s_made, 3 * h + j + 1)
                    n = S - j * P
                    src = banks[2 + j][:, 0:n] if j < 3 else banks[4][:, 256:384]
                    st.settle()
                    ins = dve.tensor_tensor(kept[:, at[j]:at[j] + n], src, decay[:, h, 0:n], ALU.mult)
                    st.do(ins, (m_made, 3 * h + min(j, 2) + 1) if j != 2 else None)

            def head_out(st, H, weight, i):
                dve = st.eng
                dve.wait_ge(r_made, H + 1)
                st.settle()
                st.do(dve.tensor_tensor(merged[:, :], banks[5][:, :], orstd[:, :], ALU.mult), (o_free, H + 1))
                st.settle()
                st.do(dve.scalar_tensor_tensor(out=merged[:, :], in0=merged[:, :], scalar=col(weight, i),
                                               in1=gate[:, H % 2, :], op0=ALU.mult, op1=ALU.mult), (mm_made, H + 1))
                st.settle()
                st.do(dve.tensor_copy(mh[:, H, :], merged[:, :]))
                st.settle()
                st.do(dve.tensor_tensor(ml[:, H, :], merged[:, :], mh[:, H, :].bitcast(F32), ALU.subtract),
                      (merged_made, H + 1))

            sg_seen = [0]

            def times_sigmoid(st, ap):
                sg_seen[0] += 1
                st.eng.wait_ge(sg_made, sg_seen[0])
                st.settle()
                st.do(st.eng.tensor_tensor(ap, ap, sg[:, :], ALU.mult), (sg_used, sg_seen[0]))

            def rotate(st, h, u):
                dve, r = st.eng, rot[:, h % 2, u, :]
                dve.wait_ge(sw_in[u], 32 * (h + 1))
                st.settle()
                st.do(dve.tensor_tensor(r, raw[:, u, :], cos[:, :], ALU.mult))
                st.settle()
                st.do(dve.tensor_tensor(sw[:, u, :], sw[:, u, :], sin[:, :], ALU.mult))
                st.settle()
                st.do(dve.tensor_tensor(r, r, sw[:, u, :], ALU.add), (rot_made, 2 * h + u + 1))

            def forget(st, h, i):
                dve = st.eng
                dve.wait_ge(p_free, i + 1)
                st.settle()
                st.do(dve.tensor_scalar(ez, ez, float(np.exp(np.float32(43.0))), None, ALU.min), (ezc_made, h + 1))
                dve.wait_ge(z_made, h + 1)
                st.settle()
                st.do(dve.tensor_tensor(ln_a[:, :], ln_a[:, :], ln_b[:, :], ALU.subtract))
                st.settle()
                st.do(dve.tensor_tensor_scan(cum[h % 2], reset[:, :], ln_a[:, :], 0.0, ALU.mult, ALU.add),
                      (b_made, h + 1))
                st.settle()
                st.do(dve.scalar_tensor_tensor(out=kin[h % 2], in0=ez, scalar=omlb[:, h:h + 1], in1=rs[:, :],
                                               op0=ALU.mult, op1=ALU.mult), (kin_made, h + 1))

            def halves(ap, s):
                v = ap.rearrange("p (n two s) -> p n two s", two=2, s=s)
                return v[:, :, 0, :], v[:, :, 1, :]

            def sub(st, h, li):
                dve, s, g = st.eng, 1 << (li - 1), 7 * h + li - 1
                left, right = halves(cum[h % 2], s)
                dl, dr = halves(diff[:, g % 2, :], s)
                end = left[:, :, s - 1:s].broadcast_to(list(left.shape))
                st.settle()
                st.do(dve.tensor_tensor(dl, end, left, ALU.subtract))
                st.settle()
                st.do(dve.tensor_tensor(dr, right, end, ALU.subtract), (d_made, g + 1))

            def mul(st, h, li):
                dve, s, g = st.eng, 1 << (li - 1), 7 * h + li - 1
                dl, dr = halves(diff[:, g % 2, :], s)
                ql, qr = halves(qk[:, g % 2, :], s)
                dve.wait_ge(e_made, g + 1)
                st.settle()
                st.do(dve.tensor_tensor(ql, halves(kin[h % 2], s)[0], dl, ALU.mult))
                st.settle()
                st.do(dve.tensor_tensor(qr, halves(qin[h % 2], s)[1], dr, ALU.mult), (qk_made, g + 1))

            def keep_level(st, h, li):
                dve, f = st.eng, 8 * h + li
                dve.wait_ge(l_made, f + 1)
                out = near.rearrange("p (c i) -> p c i", c=4)
                src = banks[2 + f % 2][:, :].rearrange("p (c i) -> p c i", c=4)
                st.settle()
                if li == 0:
                    dve.wait_ge(o_made, HEADS + h)
                    own = keep["eye"][:, :].unsqueeze(1).broadcast_to([P, 4, P])
                    ins = dve.tensor_tensor(out, src, own, ALU.mult)
                else:
                    own = masks[:, li - 1, :].unsqueeze(1).broadcast_to([P, 4, P])
                    ins = dve.copy_predicated(out, own, src)
                st.do(ins, (l_free, f + 1))

            def far_muls(st, h):
                dve, k, q = st.eng, kin[h % 2], qin[h % 2]
                dve.wait_ge(ex_made, h + 1)
                if h:
                    dve.wait_ge(far6_made, h)
                st.settle()
                st.do(dve.tensor_tensor(kx[:, 0:384], k[:, 0:384], ek[:, :], ALU.mult))
                st.settle()
                st.do(dve.tensor_tensor(qx[:, 0:256], q[:, 128:384], eq[:, 0:256], ALU.mult))
                st.settle()
                st.do(dve.tensor_tensor(qx[:, 384:512], q[:, 384:512], eq[:, 256:384], ALU.mult))
                st.settle()
                st.do(dve.tensor_scalar(kx[:, 384:512], kx[:, 0:128], eb[:, 0:1], None, ALU.mult))
                st.settle()
                st.do(dve.tensor_scalar(qx[:, 256:384], qx[:, 384:512], eb[:, 1:2], None, ALU.mult), (fx_made, h + 1))

            @block.vector
            def _(dve):
                st = Steps(dve, own_v)
                norm.dve_sums(st)
                dve.wait_ge(par_in, 16)
                st.settle()
                st.do(dve.tensor_scalar(scale1[:, :], keep["mod_pre"][:, KD:2 * KD], 1.0, None, ALU.add))
                st.settle()
                st.do(dve.tensor_tensor(scale1[:, :], scale1[:, :], cols("norm1"), ALU.mult), (par_made, 1))
                norm.dve_normalise(st, x)
                lower_bounds(st)
                st.settle()
                st.do(dve.tensor_scalar(omlb[:, :], lbt[:, :], -1.0, 1.0, ALU.mult, ALU.add), (par_made, 2))
                dve.wait_ge(const_in, 80)
                for G in range(9):
                    J = G - 1
                    for u in range(3):
                        i = 3 * G + u
                        for k in range(32):
                            if ada_at(k) == i:
                                ada.add(st, k)
                        if 0 <= J < 4:
                            if u == 1:
                                mask_scores(st, J)
                            if u == 2:
                                head_out(st, J, "ret_w", J)
                        if J >= 4:
                            h = J - 4
                            if u == 0:
                                sub(st, h, 3)
                                keep_level(st, h, 0)
                                sub(st, h, 4)
                                keep_level(st, h, 1)
                                mul(st, h, 3)
                                sub(st, h, 5)
                                keep_level(st, h, 2)
                                mul(st, h, 4)
                            if u == 1:
                                keep_level(st, h, 3)
                                mul(st, h, 5)
                                sub(st, h, 6)
                                far_muls(st, h)
                                keep_level(st, h, 4)
                                sub(st, h, 7)
                                mul(st, h, 6)
                                keep_level(st, h, 5)
                                mul(st, h, 7)
                                keep_level(st, h, 6)
                            if u == 2:
                                keep_level(st, h, 7)
                                head_out(st, J, "hgrn_w", h)
                        if G == 8:
                            continue
                        if u == 2:
                            if G >= 4:
                                mul(st, G - 4, 2)
                            times_sigmoid(st, gate[:, G % 2, :])
                        elif G < 4:
                            rotate(st, G, u)
                        elif u == 0:
                            forget(st, G - 4, i)
                        else:
                            times_sigmoid(st, qin[(G - 4) % 2])
                            sub(st, G - 4, 1)
                            sub(st, G - 4, 2)
                            mul(st, G - 4, 1)
                dve.wait_ge(ada.used, 32)
                st.settle()
                st.do(dve.tensor_tensor(keep["mod"][:, :], banks[7][:, 0:32], cols("ada_b"), ALU.add))
                for n in range(KD):
                    dve.wait_ge(ws.used, first_out + n + 1)
                    st.settle()
                    st.do(dve.scalar_tensor_tensor(out=x[:, n, :], in0=banks[n % 2][:, :],
                                                   scalar=keep["mod"][:, n:n + 1], in1=x[:, n, :],
                                                   op0=ALU.mult, op1=ALU.add), (y_free, n + 1))

        sc.clear()


def ffn_a(nc, io, keep, l):
    with ExitStack() as ctx:
        sc = Scope(nc, ctx, "fa")
        x = keep["x"]
        banks = [sc.ps(f"bank{i}", [P, 512]) for i in range(8)]
        par = sc.sb("par", [P, A_N])
        hh, hl = sc.sb("h_hi", [P, KD, S], F32R), sc.sb("h_lo", [P, KD, S], F32R)
        yh, yl = sc.sb("y_hi", [P, KF, S], F32R), sc.sb("y_lo", [P, KF, S], F32R)
        units = [(io["a_wgv"][l, n], D) for n in range(2 * KF)]
        units += down_units(io["a_wd"], l)
        ws = Weights(sc, units)
        ada = Ada(sc, banks[7], keep["c_act"], keep["ones"], [io["ada"][l, 32 + n] for n in range(16)], slots=1)
        a_in = sc.sb("a_in", [P, 2, S + 2])
        conv, y = sc.sb("conv", [P, 2, S]), sc.sb("y", [P, 2, S])
        scale2 = sc.sb("scale2", [P, KD])
        norm = Norm(sc, hh, hl, conv, y, sc.sb("nh", [P, 2, S]), sc.sb("nacc", [P, S]), sc.sb("nrstd", [P, S]))
        par_in, par_made = sc.sem("par_in"), sc.sem("par_made")
        a_made, conv_made, silu_made, y_made, v_free = (sc.sem("a_made"), sc.sem("conv_made"), sc.sem("silu_made"),
                                                        sc.sem("y_made"), sc.sem("v_free"))
        lo_made, out_free = sc.sem("y_lo_made"), sc.sem("out_free")
        own_a, own_v, own_p = sc.sem("act_own"), sc.sem("dve_own"), sc.sem("pool_own")

        def col(name, i):
            return par[:, A_AT[name][0] + i:A_AT[name][0] + i + 1]

        with nc.Block() as block:
            @block.sync
            def _(sp):
                sp.dma_start(par[:, :], io["a_par"][l]).then_inc(par_in, 16)
                for n in range(len(units)):
                    ws.load(sp, n)
                    if n >= 4 and n % 2 == 0 and (n - 4) // 2 < 16:
                        ada.load(sp, (n - 4) // 2)

            @block.gpsimd
            def _(pool):
                st = Steps(pool, own_p)
                norm.pool(st, ws)
                for n in range(2, len(units)):
                    ws.low(st, n)
                    if n >= 3 and n % 2 == 1 and (n - 3) // 2 < 16:
                        ada.scale(st, (n - 3) // 2)

            @block.scalar
            def _(act):
                st = Steps(act, own_a)
                norm.act_sums(st, x, banks[6], keep["eps"][:, 0:1], ws)
                act.wait_ge(par_made, 1)
                norm.act_affine(st, scale2, keep["mod"][:, KD:2 * KD])
                for j in range(KF + 1):
                    if j < KF:
                        for u in range(2):
                            ws.high(st, 2 * j + u + 1 if 2 * j + u + 1 < 2 * KF else 0)
                        act.wait_ge(ws.used, 2 * j + 1)
                        if j >= 2:
                            act.wait_ge(conv_made, j - 1)
                        st.settle()
                        st.do(act.activation(a_in[:, j % 2, 2:S + 2], banks[j % 2][:, :], ACT.Copy), (a_made, j + 1))
                    if j >= 1:
                        act.wait_ge(conv_made, j)
                        st.settle()
                        st.do(act.activation(conv[:, (j - 1) % 2, :], conv[:, (j - 1) % 2, :], ACT.Silu,
                                             bias=col("conv_b", j - 1)), (silu_made, j))
                ws.high(st, len(units) - 1)

            @block.tensor
            def _(pe):
                norm.pe(pe, banks[6], keep["ones"])
                for j in range(KF):
                    if j >= 2:
                        pe.wait_ge(a_made, j - 1)
                    ws.project(pe, banks[j % 2][:, :], hh, hl, ready=norm.ready if j == 0 else None)
                    if j >= 2:
                        pe.wait_ge(v_free, j - 1)
                    ws.project(pe, banks[2 + j % 2][:, :], hh, hl)
                    if 2 <= j < 18:
                        ada.product(pe)
                for n in range(KD):
                    if n >= 2:
                        pe.wait_ge(out_free, n - 1)
                    for part, k0 in enumerate(range(0, KF, KD)):
                        ws.project(pe, banks[4 + n % 2][:, :], yh, yl, k0=k0, first=part == 0, last=part == 2,
                                   ready=lo_made if n == 0 else None)

            @block.vector
            def _(dve):
                st = Steps(dve, own_v)
                norm.dve_sums(st)
                dve.wait_ge(par_in, 16)
                st.settle()
                st.do(dve.tensor_scalar(scale2[:, :], keep["mod"][:, 2 * KD:3 * KD], 1.0, None, ALU.add))
                st.settle()
                st.do(dve.tensor_tensor(scale2[:, :], scale2[:, :], par[:, A_AT["norm2"][0]:A_AT["norm2"][1]], ALU.mult),
                      (par_made, 1))
                norm.dve_normalise(st, x)
                st.settle()
                st.do(dve.memset(a_in[:, :, 0:2], 0.0))
                for j in range(KF + 1):
                    if 2 <= j < 18:
                        ada.add(st, j - 2)
                    if j < KF:
                        b = j % 2
                        dve.wait_ge(a_made, j + 1)
                        st.settle()
                        st.do(dve.tensor_scalar(conv[:, b, :], a_in[:, b, 0:S], col("conv0", j), None, ALU.mult))
                        st.settle()
                        st.do(dve.scalar_tensor_tensor(out=conv[:, b, :], in0=a_in[:, b, 1:S + 1], scalar=col("conv1", j),
                                                       in1=conv[:, b, :], op0=ALU.mult, op1=ALU.add))
                        st.settle()
                        st.do(dve.scalar_tensor_tensor(out=conv[:, b, :], in0=a_in[:, b, 2:S + 2], scalar=col("conv2", j),
                                                       in1=conv[:, b, :], op0=ALU.mult, op1=ALU.add), (conv_made, j + 1))
                    if j >= 1:
                        i = j - 1
                        dve.wait_ge(silu_made, j)
                        dve.wait_ge(ws.used, 2 * j)
                        st.settle()
                        st.do(dve.tensor_tensor(y[:, i % 2, :], banks[2 + i % 2][:, :], conv[:, i % 2, :], ALU.mult),
                              (v_free, j))
                        st.settle()
                        st.do(dve.tensor_copy(yh[:, i, :], y[:, i % 2, :]))
                        st.settle()
                        st.do(dve.tensor_tensor(yl[:, i, :], y[:, i % 2, :], yh[:, i, :].bitcast(F32), ALU.subtract),
                              (lo_made, j))
                dve.wait_ge(ada.used, 16)
                st.settle()
                st.do(dve.tensor_tensor(keep["mod_pre"][:, :], banks[7][:, 0:16],
                                        par[:, A_AT["ada_b_next"][0]:A_AT["ada_b_next"][1]], ALU.add))
                for n in range(KD):
                    dve.wait_ge(ws.used, 2 * KF + 3 * (n + 1))
                    st.settle()
                    st.do(dve.scalar_tensor_tensor(out=x[:, n, :], in0=banks[4 + n % 2][:, :],
                                                   scalar=keep["mod"][:, 3 * KD + n:3 * KD + n + 1], in1=x[:, n, :],
                                                   op0=ALU.mult, op1=ALU.add), (out_free, n + 1))
        sc.clear()


def down_units(w, l):
    out = []
    for n in range(KD):
        for k0 in range(0, KF, KD):
            k1 = min(k0 + KD, KF)
            out.append((w[l, n][:, k0 * P:k1 * P], (k1 - k0) * P))
    return out


PAIRS = 8
C = 64
NC = S // C
INV_LEVELS = (2, 4, 8, 16, 32)


def rope_tables(nc, io, keep):
    with ExitStack() as ctx:
        sc = Scope(nc, ctx, "rt")
        pos_i, ang = sc.sb("pos_i", [P, S], I32), sc.sb("ang", [P, S])
        turns, col = sc.sb("turns", [P, S]), sc.sb("col", [P, 2])
        wrap = sc.sb("wrap", [P, S])
        in_, own_v, ready, made = sc.sem("in"), sc.sem("own_v"), sc.sem("ready"), sc.sem("made")
        two_pi = 2.0 * np.pi
        hi = np.float32(6.28125)
        mid = np.float32(np.round((two_pi - float(hi)) * 2.0 ** 20) / 2.0 ** 20)
        low = np.float32(two_pi - float(hi) - float(mid))
        magic = float(np.float32(1.5 * 2 ** 23))
        pi = float(np.float32(3.1415925))
        with nc.Block() as block:
            @block.sync
            def _(sp):
                sp.dma_start(pos_i[:, :], io["b_pos"]).then_inc(in_, 16)
                sp.dma_start(col[:, :], io["b_freq"]).then_inc(in_, 16)

            @block.vector
            def _(dve):
                st = Steps(dve, own_v)

                def op(ins):
                    st.do(ins)
                    st.settle()
                dve.wait_ge(in_, 32)
                op(dve.tensor_copy(ang[:, :], pos_i[:, :]))
                op(dve.tensor_scalar(ang[:, :], ang[:, :], col[:, 0:1], None, ALU.mult))
                op(dve.tensor_scalar(turns[:, :], ang[:, :], 1.0 / two_pi, None, ALU.mult))
                op(dve.tensor_scalar(turns[:, :], turns[:, :], magic, None, ALU.add))
                op(dve.tensor_scalar(turns[:, :], turns[:, :], -magic, None, ALU.add))
                for part in (hi, mid, low):
                    op(dve.scalar_tensor_tensor(out=ang[:, :], in0=turns[:, :], scalar=-float(part), in1=ang[:, :],
                                                op0=ALU.mult, op1=ALU.add))
                op(dve.tensor_scalar(turns[:, :], ang[:, :], float(np.pi / 2), None, ALU.add))
                op(dve.tensor_scalar(wrap[:, :], turns[:, :], pi, two_pi, ALU.is_gt, ALU.mult))
                op(dve.tensor_tensor(turns[:, :], turns[:, :], wrap[:, :], ALU.subtract))
                op(dve.tensor_scalar(turns[:, :], turns[:, :], pi, -pi, ALU.min, ALU.max))
                st.do(dve.tensor_scalar(ang[:, :], ang[:, :], pi, -pi, ALU.min, ALU.max), (ready, 1))
                dve.wait_ge(made, 2)
                op(dve.tensor_scalar(keep["b_sin"][:, :], keep["b_sin"][:, :], col[:, 1:2], None, ALU.mult))

            @block.scalar
            def _(act):
                act.wait_ge(ready, 1)
                act.activation(keep["b_cos"][:, :], turns[:, :], ACT.Sin).then_inc(made, 1)
                act.activation(keep["b_sin"][:, :], ang[:, :], ACT.Sin).then_inc(made, 1)
        sc.clear()


def sigmoid_steps(st, dst, src, signal, half, bias=0.0, free=None):
    act = st.eng
    st.settle()
    st.do(act.activation(dst, src, ACT.Tanh, scale=0.5, bias=bias), free)
    st.settle()
    st.do(act.activation(dst, dst, ACT.Identity, scale=0.5, bias=half), signal)


def b_columns(par):
    def col(name, i):
        return par[:, B_AT[name][0] + i:B_AT[name][0] + i + 1]
    return col


def attention_b(nc, io, keep, l, hh, hl, mixed):
    with ExitStack() as ctx:
        sc = Scope(nc, ctx, "at")
        x = keep["x"]
        half = keep["eps"][:, 3:4]
        banks = [sc.ps(f"bank{i}", [P, 512]) for i in range(8)]
        par = sc.sb("par", [P, B_N])
        oh, ol = sc.sb("o_hi", [P, KD, S], F32R), sc.sb("o_lo", [P, KD, S], F32R)
        units = [(io["b_wk"][l, n], D) for n in range(2)] + [(io["b_wv"][l, n], D) for n in range(2)]
        units += [(io["b_wq"][l, n], D) for n in range(8)] + [(io["b_wga"][l, n], D) for n in range(8)]
        units += [(io["b_woa"][l, n], D) for n in range(8)]
        ws = Weights(sc, units)
        raw, sw, rot = sc.sb("raw", [P, 2, S]), sc.sb("sw", [P, 2, S]), sc.sb("rot", [P, 2, S])
        kpad = sc.sb("kpad", [P, 2, P + S])
        v_tok = sc.sb("v_tok", [P, 4, 256])
        s = sc.sb("s", [P, 3, 1024])
        pt = sc.sb("pt", [P, 3, 1024])
        band = sc.sb("band", [P, 768])
        sink = sc.sb("sink", [P, 32])
        mx, nmx, es, den = (sc.sb("mx", [P, 3, 4]), sc.sb("nmx", [P, 3, 4]), sc.sb("es", [P, 3, 4]),
                            sc.sb("den", [P, 3, 4]))
        acc, rstd = sc.sb("acc", [P, S]), sc.sb("rstd", [P, S])
        norm = Norm(sc, hh, hl, raw, sw, rot, acc, rstd)
        par_in, const_in, par_made = sc.sem("par_in"), sc.sem("const_in"), sc.sem("par_made")
        p_free, v_used = sc.sem("p_free"), sc.sem("v_used")
        sw_in = [sc.sem("sw_in0"), sc.sem("sw_in1")]
        rot_made, s_made, s_free = sc.sem("rot_made"), sc.sem("s_made"), sc.sem("s_free")
        stat_made, exp_made, p_made = sc.sem("stat_made"), sc.sem("exp_made"), sc.sem("p_made")
        t_made, t_kept, o_made, o_free = sc.sem("t_made"), sc.sem("t_kept"), sc.sem("o_made"), sc.sem("o_free")
        oh_made, ol_made, ga_made, y_free = sc.sem("oh_made"), sc.sem("ol_made"), sc.sem("ga_made"), sc.sem("y_free")
        own_a, own_v, own_p = sc.sem("own_a"), sc.sem("own_v"), sc.sem("own_p")
        slot_unit = [4 + 2 + t // 2 for t in range(20)]
        T = 16

        with nc.Block() as block:
            @block.sync
            def _(sp):
                sp.dma_start(par[:, :], io["b_par"][l]).then_inc(par_in, 16)
                for n in range(len(units)):
                    ws.load(sp, n)
                    if n == 1:
                        sp.dma_start(band[:, :], io["b_band"]).then_inc(const_in, 16)
                        sp.dma_start(sink[:, :], io["b_sink"][l]).then_inc(const_in, 16)

            @block.gpsimd
            def _(pool):
                st = Steps(pool, own_p)
                norm.pool(st, ws)
                for n in range(2, len(units)):
                    ws.low(st, n)

            @block.scalar
            def _(act):
                st = Steps(act, own_a)

                def exps(t):
                    b = t % 3
                    act.wait_ge(stat_made, t + 1)
                    for i in range(4):
                        st.settle()
                        a = s[:, b, 256 * i:256 * (i + 1)]
                        st.do(act.activation(a, a, ACT.Exp, bias=nmx[:, b, i:i + 1], accum_out=den[:, b, i:i + 1]))
                    st.settle()
                    st.do(act.activation(es[:, b, :], es[:, b, :], ACT.Exp), (exp_made, t + 1))

                def keep_transposed(t):
                    act.wait_ge(t_made, t + 1)
                    if t >= 3:
                        act.wait_ge(o_made, t - 2)
                    for i in range(2):
                        st.settle()
                        st.do(act.activation(pt[:, t % 3, 512 * i:512 * (i + 1)], banks[4 + i][:, :], ACT.Copy),
                              (t_kept, 2 * t + i + 1))

                def slot(t):
                    if 2 <= t < T + 2:
                        keep_transposed(t - 2)
                    if t < T:
                        exps(t)
                    if t >= 5 and t % 2 == 1:
                        p = (t - 5) // 2
                        act.wait_ge(o_made, 2 * p + 2)
                        st.settle()
                        st.do(act.activation(oh[:, p, :], banks[6][:, :], ACT.Copy), (oh_made, p + 1))

                norm.act_sums(st, x, banks[6], keep["eps"][:, 0:1], ws)
                act.wait_ge(par_in, 16)
                norm.act_affine(st, par[:, B_AT["norm_mix_pre"][0]:B_AT["norm_mix_pre"][1]], None)
                nr = 0
                for n in range(20):
                    ws.high(st, n + 1)
                    for t in range(20):
                        if slot_unit[t] == n:
                            slot(t)
                    act.wait_ge(ws.used, n + 1)
                    if n in (2, 3):
                        if n == 3:
                            for t in range(4):
                                st.settle()
                                st.do(act.activation(v_tok[:, t, :], banks[2 + t][:, 0:256], ACT.Copy), (v_used, t + 1))
                        continue
                    i = n if n < 2 else n - 2
                    if n < 12:
                        b = nr % 2
                        if nr >= 2:
                            act.wait_ge(rot_made, nr - 1)
                        st.settle()
                        st.do(act.activation(raw[:, b, :], banks[i % 2][:, :], ACT.Copy), (p_free, i + 1))
                        st.settle()
                        for q in range(4):
                            act.dma_start(sw[32 * q:32 * q + 32, b, :], raw[32 * (q ^ 1):32 * (q ^ 1) + 32, b, :])\
                                .then_inc(sw_in[b], 16)
                        nr += 1
                    else:
                        m = n - 12
                        sigmoid_steps(st, mixed[:, m, :], banks[i % 2][:, :], (ga_made, m + 1), half, free=(p_free, i + 1))
                ws.high(st, len(units) - 1)

            @block.tensor
            def _(pe):
                def slot(t):
                    if t < T:
                        p, f = t // 2, t % 2
                        kb = p // 4
                        if f == 0:
                            pe.wait_ge(rot_made, 2 + p + 1)
                        if t >= 1:
                            pe.wait_ge(s_free, 2 * t)
                        for g in range(2):
                            rows = slice(64 * g, 64 * g + 64)
                            for j in range(2):
                                ib = 2 * f + j
                                mm = pe.matmul(banks[2 + g][:, 256 * j:256 * (j + 1)], rot[rows, p % 2, ib * P:(ib + 1) * P],
                                               kpad[rows, kb, ib * P:(ib + 2) * P], start=True, stop=True)
                            mm.then_inc(s_made, 1)
                    if 2 <= t < T + 2:
                        u = t - 2
                        pe.wait_ge(p_made, u + 1)
                        if u:
                            pe.wait_ge(t_kept, 2 * u)
                        for i in range(8):
                            mm = pe.transpose(banks[4 + i // 4][:, (i % 4) * P:(i % 4 + 1) * P],
                                              s[:, u % 3, i * P:(i + 1) * P], keep["eye"][:, :])
                        mm.then_inc(t_made, 1)
                    if t >= 4:
                        u = t - 4
                        p, f = u // 2, u % 2
                        kb = p // 4
                        if f == 0 and p:
                            pe.wait_ge(oh_made, p)
                            pe.wait_ge(ol_made, p)
                        for g in range(2):
                            pe.wait_ge(t_kept, 2 * u + g + 1)
                            for j in range(2):
                                ib = 2 * f + j
                                for e in range(2):
                                    if ib == 0 and e == 0:
                                        continue
                                    a = ((g * 2 + j) * 2 + e) * P
                                    mm = pe.matmul(banks[6][64 * g:64 * g + 64, ib * P:(ib + 1) * P],
                                                   v_tok[:, ib + e - 1, (2 * kb + g) * 64:(2 * kb + g + 1) * 64],
                                                   pt[:, u % 3, a:a + P], start=e == 0 or ib == 0, stop=e == 1)
                        mm.then_inc(o_made, 1)

                norm.pe(pe, banks[6], keep["ones"])
                for n in range(20):
                    if n in (2, 3):
                        ws.project_tokens(pe, [banks[2 + t][:, 0:256] for t in range(4)], hh, hl, n - 2, 256)
                        if n == 3:
                            pe.wait_ge(v_used, 4)
                        continue
                    i = n if n < 2 else n - 2
                    if i >= 2:
                        pe.wait_ge(p_free, i - 1)
                    ts = [t for t in range(20) if slot_unit[t] == n]

                    def between(k):
                        if k % 4 == 3 and k // 4 < len(ts):
                            slot(ts[k // 4])
                    ws.project(pe, banks[i % 2][:, :], hh, hl, between=between, ready=norm.ready if n == 0 else None)
                pe.wait_ge(ol_made, 8)
                for m in range(8):
                    if m >= 2:
                        pe.wait_ge(y_free, m - 1)
                    ws.project(pe, banks[2 + m % 2][:, :], oh, ol)

            @block.vector
            def _(dve):
                st = Steps(dve, own_v)

                def normalise(t):
                    b = t % 3
                    dve.wait_ge(exp_made, t + 1)
                    st.settle()
                    st.do(dve.tensor_tensor(den[:, b, :], den[:, b, :], es[:, b, :], ALU.add))
                    st.settle()
                    st.do(dve.reciprocal(den[:, b, :], den[:, b, :]))
                    st.settle()
                    a = s[:, b, :].rearrange("p (i j) -> p i j", i=4)
                    st.do(dve.tensor_tensor(a, a, den[:, b, :].unsqueeze(2).broadcast_to([P, 4, 256]), ALU.mult),
                          (p_made, t + 1))

                def stats(t):
                    p, f, b = t // 2, t % 2, t % 3
                    if t >= 3:
                        dve.wait_ge(t_made, t - 2)
                    for g in range(2):
                        dve.wait_ge(s_made, 2 * t + g + 1)
                        st.settle()
                        st.do(dve.scalar_tensor_tensor(out=s[:, b, 512 * g:512 * (g + 1)], in0=banks[2 + g][:, :],
                                                       scalar=64.0 ** -0.5, in1=band[:, 256 * f:256 * f + 512],
                                                       op0=ALU.mult, op1=ALU.add), (s_free, 2 * t + g + 1))
                    st.settle()
                    st.do(dve.tensor_reduce(mx[:, b, :], s[:, b, :].rearrange("p (i j) -> p i j", i=4), AX.X, ALU.max))
                    st.settle()
                    st.do(dve.tensor_tensor(mx[:, b, :], mx[:, b, :], sink[:, 4 * p:4 * p + 4], ALU.max))
                    st.settle()
                    st.do(dve.tensor_tensor(es[:, b, :], sink[:, 4 * p:4 * p + 4], mx[:, b, :], ALU.subtract))
                    st.settle()
                    st.do(dve.tensor_scalar(nmx[:, b, :], mx[:, b, :], -1.0, None, ALU.mult), (stat_made, t + 1))

                def slot(t):
                    if t < T:
                        stats(t)
                    if 1 <= t <= T:
                        normalise(t - 1)
                    if t >= 5 and t % 2 == 1:
                        p = (t - 5) // 2
                        dve.wait_ge(oh_made, p + 1)
                        st.settle()
                        st.do(dve.tensor_tensor(ol[:, p, :], banks[6][:, :], oh[:, p, :].bitcast(F32), ALU.subtract),
                              (ol_made, p + 1))

                norm.dve_sums(st)
                norm.dve_normalise(st, x)
                st.settle()
                st.do(dve.memset(kpad[:, :, 0:P], 0.0))
                dve.wait_ge(const_in, 32)

                def rotate(nr):
                    b = nr % 2
                    r = kpad[:, nr, P:P + S] if nr < 2 else rot[:, nr % 2, :]
                    if nr >= 4:
                        dve.wait_ge(s_made, 4 * (nr - 4) + 4)
                    dve.wait_ge(sw_in[b], 64 * (nr // 2 + 1))
                    st.settle()
                    st.do(dve.tensor_tensor(r, raw[:, b, :], keep["b_cos"][:, :], ALU.mult))
                    st.settle()
                    st.do(dve.tensor_tensor(sw[:, b, :], sw[:, b, :], keep["b_sin"][:, :], ALU.mult))
                    st.settle()
                    st.do(dve.tensor_tensor(r, r, sw[:, b, :], ALU.add), (rot_made, nr + 1))

                for n in range(20):
                    ts = [t for t in range(20) if slot_unit[t] == n]
                    if ts:
                        slot(ts[0])
                    if n - 1 in (0, 1) or 4 <= n - 1 < 12:
                        rotate(n - 1 if n < 4 else n - 3)
                    for t in ts[1:]:
                        slot(t)
                for m in range(8):
                    dve.wait_ge(ws.used, 20 + m + 1)
                    dve.wait_ge(ga_made, m + 1)
                    st.settle()
                    st.do(dve.tensor_tensor(mixed[:, m, :], mixed[:, m, :], banks[2 + m % 2][:, :], ALU.mult),
                          (y_free, m + 1))
        sc.clear()


def rwkv_b(nc, io, keep, l, hh, hl, y_all):
    with ExitStack() as ctx:
        sc = Scope(nc, ctx, "rw")
        half = keep["eps"][:, 3:4]
        banks = [sc.ps(f"bank{i}", [P, 512]) for i in range(8)]
        par = sc.sb("par", [P, B_N])
        col = b_columns(par)
        units = [(io["b_wlow"][l, n], D) for n in range(3)]
        units += [(io["b_wrkv"][l, n], D) for n in range(3 * PAIRS)]
        ws = Weights(sc, units, raw=3)
        z = sc.sb("z", [P, 2, S + 1])
        r, ks, v, kp = sc.sb("r", [P, S]), sc.sb("ks", [P, S]), sc.sb("v", [P, S]), sc.sb("kp", [P, S])
        lw, a, kt, cum = sc.sb("lw", [P, S]), sc.sb("a", [P, S]), sc.sb("kt", [P, S]), sc.sb("cum", [P, S])
        e0, e1, kn, yq = sc.sb("e0", [P, S]), sc.sb("e1", [P, S]), sc.sb("kn", [P, S]), sc.sb("yq", [P, S])
        gg, bonus = sc.sb("gg", [P, 2, S]), sc.sb("bonus", [P, 2, S])
        wa, gd = sc.sb("wa", [P, S]), sc.sb("gd", [P, 2, S])
        lr, g2 = sc.sb("lr", [P, 2, P]), sc.sb("g2", [P, 2, 2, P])
        halves = sc.sb("halves", [P, 16])
        at_, rt = sc.sb("at", [P, 2, S]), sc.sb("rt", [P, 2, S])
        mak, mrb, mrk, xt = sc.sb("mak", [P, S]), sc.sb("mrb", [P, S]), sc.sb("mrk", [P, S]), sc.sb("xt", [P, S])
        vt, bt, ktt = sc.sb("vt", [P, S]), sc.sb("bt", [P, S]), sc.sb("ktt", [P, S])
        mabt, xx, pp, ct = sc.sb("mabt", [P, S]), sc.sb("xx", [P, S]), sc.sb("pp", [P, S]), sc.sb("ct", [P, S])
        ec = sc.sb("ec", [P, 2, NC])
        rhs, uu, state = sc.sb("rhs", [P, C]), sc.sb("uu", [P, C]), sc.sb("state", [P, C])
        lm = sc.sb("lm", [P, 10, C])
        bones, reset = sc.sb("bones", [P, P]), sc.sb("reset", [P, S])
        par_in, const_in, low_in, par_made = sc.sem("par_in"), sc.sem("const_in"), sc.sem("low_in"), sc.sem("par_made")
        p_free, pd_free = sc.sem("p_free"), sc.sem("pd_free")
        pn_free = sc.sem("pn_free")
        z_free = sc.sem("z_free")
        wa_made, gd_made, lr_made, g_made = sc.sem("wa_made"), sc.sem("gd_made"), sc.sem("lr_made"), sc.sem("g_made")
        wsig, asig, b_made, c_made = sc.sem("wsig"), sc.sem("asig"), sc.sem("b_made"), sc.sem("c_made")
        enb_made, eb_made, ebm_made = sc.sem("enb_made"), sc.sem("eb_made"), sc.sem("ebm_made")
        sq_made, ssq_made, rn_made, rt_made = sc.sem("sq_made"), sc.sem("ssq_made"), sc.sem("rn_made"), sc.sem("rt_made")
        rk_made, bon_made = sc.sem("rk_made"), sc.sem("bon_made")
        bbar_made, kbar_made = sc.sem("bbar_made"), sc.sem("kbar_made")
        f_made, f_free, tr_made, tr_kept = sc.sem("f_made"), sc.sem("f_free"), sc.sem("tr_made"), sc.sem("tr_kept")
        x_made, xt_made, c_ready = sc.sem("x_made"), sc.sem("xt_made"), sc.sem("c_ready")
        cx_made, cx_kept, xcx_made, xcxt_made = (sc.sem("cx_made"), sc.sem("cx_kept"), sc.sem("xcx_made"),
                                                 sc.sem("xcxt_made"))
        ch_made, ch_kept, y_kept = sc.sem("ch_made"), sc.sem("ch_kept"), sc.sem("y_kept")
        mean_made, ysq_made, var_made, yr_made, y_done = (sc.sem("mean_made"), sc.sem("ysq_made"), sc.sem("var_made"),
                                                          sc.sem("yr_made"), sc.sem("y_done"))
        low_sig = sc.sem("low_sig")
        own_a, own_v, own_p = sc.sem("own_a"), sc.sem("own_v"), sc.sem("own_p")

        readers = {"A": p_free, "V": pd_free, "N": pn_free}
        order, place = [], {}
        for n in range(3):
            place["low", n] = len(order)
            order.append("A")
        place["k", 0] = len(order)
        order.append("A")
        for p in range(PAIRS + 1):
            for name, q, who in (("w", p, "A"), ("a", p, "A"), ("r", p, "A"), ("ssq", p, "V"), ("v", p, "A"),
                                 ("g", p, "A"), ("bonus", p, "V"), ("mean", p, "V"), ("k", p + 1, "A"), ("var", p, "N")):
                if (p >= 1 if name in ("mean", "var") else q < PAIRS):
                    place[name, q] = len(order)
                    order.append(who)

        def read(name, p):
            e = place[name, p]
            return readers[order[e]], order[:e + 1].count(order[e])

        heads = (slice(0, C), slice(C, 2 * C))

        def cut(c):
            return slice(c * C, (c + 1) * C)

        def chunks(ap):
            return ap.rearrange("p (c i) -> p c i", i=C)

        def each_chunk(mask):
            return mask.unsqueeze(1).broadcast_to([P, NC, C])

        with nc.Block() as block:
            @block.sync
            def _(sp):
                sp.dma_start(par[:, :], io["b_par"][l]).then_inc(par_in, 16)
                for n in range(len(units)):
                    ws.load(sp, n)
                    if n == 1:
                        sp.dma_start(lm[:, :, :], io["b_lm"]).then_inc(const_in, 16)
                        sp.dma_start(bones[:, :], io["b_bones"]).then_inc(const_in, 16)
                        sp.dma_start(reset[:, :], io["b_reset"]).then_inc(const_in, 16)
                    if n >= 2 and (n - 2) % 3 == 0 and (n - 2) // 3 < PAIRS:
                        p = (n - 2) // 3
                        if p >= 2:
                            sp.wait_ge(g_made, p - 1)
                        sp.dma_start(lr[:, p % 2, :], io["b_wlr"][l, p]).then_inc(low_in, 16)
                        sp.dma_start(g2[:, p % 2, :, :], io["b_wg2"][l, p]).then_inc(low_in, 16)

            @block.gpsimd
            def _(pool):
                st = Steps(pool, own_p)
                for n in range(len(units)):
                    ws.low(st, n)

            @block.tensor
            def _(pe):
                def claim(name, p):
                    e = place[name, p]
                    if e >= 2:
                        who = order[e - 2]
                        pe.wait_ge(readers[who], order[:e - 1].count(who))
                    return banks[e % 2][:, :]

                def whole(name, p, lhs, rhs_, signal):
                    pe.matmul(claim(name, p), lhs, rhs_, start=True, stop=True).then_inc(signal, 1)

                def chain(p, i):
                    b2, c, n = p % 2, i // 3, 24 * p + i
                    t = cut(c)
                    pe.wait_ge(ch_kept, n + 1)
                    if i % 3 == 0:
                        if i == 0 and p:
                            pe.wait_ge(y_kept, p)
                        if i == 0:
                            pe.wait_ge(xt_made, 6 * (p + 1))
                            pe.wait_ge(tr_kept, 12 * (p + 1))
                        for s_ in heads:
                            pe.matmul(banks[6][s_, 0:C], at_[s_, b2, t], state[s_, :], start=True, stop=False)
                            mm = pe.matmul(banks[6][s_, 0:C], mak[s_, t], vt[s_, t], start=False, stop=True)
                        mm.then_inc(ch_made, 1)
                        for s_ in heads:
                            pe.matmul(banks[7][s_, t], state[s_, :], rt[s_, b2, t], start=True, stop=False)
                            pe.matmul(banks[7][s_, t], vt[s_, t], mrk[s_, t], start=False, stop=False)
                    elif i % 3 == 1:
                        for s_ in heads:
                            mm = pe.matmul(banks[6][s_, C:2 * C], xt[s_, t], rhs[s_, :], start=True, stop=True)
                        mm.then_inc(ch_made, 1)
                    else:
                        for s_ in heads:
                            mm = pe.matmul(banks[7][s_, t], uu[s_, :], mrb[s_, t], start=False, stop=True)
                        if c < NC - 1:
                            for s_ in heads:
                                pe.matmul(banks[6][s_, 2 * C:3 * C], bt[s_, t], uu[s_, :], start=True, stop=False)
                                mm = pe.matmul(banks[6][s_, 2 * C:3 * C], ktt[s_, t], vt[s_, t], start=False, stop=True)
                        mm.then_inc(ch_made, 1)

                def products(bank, lhs, rhs_, signal):
                    for c in range(NC):
                        for s_ in heads:
                            mm = pe.matmul(banks[bank][s_, cut(c)], lhs[s_, cut(c)], rhs_[s_, cut(c)], start=True, stop=True)
                    mm.then_inc(signal, 1)

                for n in range(3):
                    ws.project(pe, claim("low", n), hh, hl)
                ws.project(pe, claim("k", 0), hh, hl)
                for p in range(PAIRS + 1):
                    steps = iter(range(24))

                    def chain_on(count=1):
                        if p:
                            for _ in range(count):
                                chain(p - 1, next(steps))
                    if p == PAIRS:
                        chain_on(24)
                    else:
                        if p == 0:
                            pe.wait_ge(wa_made, 1)
                        pe.wait_ge(low_in, 32 * (p + 1))
                        whole("w", p, lr[0:64, p % 2, :], wa[0:64, :], lr_made)
                        chain_on()
                        whole("a", p, lr[64:128, p % 2, :], wa[64:128, :], lr_made)
                        chain_on()
                        ws.project(pe, claim("r", p), hh, hl, between=lambda k: chain_on(1 + (k == 3)))
                        pe.wait_ge(sq_made, p + 1)
                        whole("ssq", p, bones[:, :], e0[:, :], ssq_made)
                        chain_on()
                        ws.project(pe, claim("v", p), hh, hl, between=lambda k: chain_on(1 + (k in (2, 5))))
                        if p == 0:
                            pe.wait_ge(gd_made, 2)
                        out = claim("g", p)
                        pe.matmul(out, g2[:, p % 2, 0, :], gd[:, 0, :], start=True, stop=False)
                        chain_on()
                        pe.matmul(out, g2[:, p % 2, 1, :], gd[:, 1, :], start=False, stop=True).then_inc(g_made, 1)
                        chain_on()
                        pe.wait_ge(rk_made, p + 1)
                        whole("bonus", p, bones[:, :], r[:, :], bon_made)
                        b2 = p % 2
                        for j, (lhs, rh) in enumerate(((a, at_[:, b2, :]), (at_[:, b2, :], a), (kt, at_[:, b2, :]),
                                                       (a, rt[:, b2, :]), (kt, rt[:, b2, :]))):
                            f = 5 * p + j
                            if j >= 2:
                                pe.wait_ge(f_free, f - 1)
                            elif p:
                                pe.wait_ge(cx_kept, 5 * p)
                            products(2 + j % 2, lhs, rh, f_made)
                        pe.wait_ge(z_free, 3 + 3 * p + 3)
                        pe.wait_ge(kbar_made, p + 1)
                        for j, src in enumerate((v, e0, e1)):
                            if j == 1:
                                pe.wait_ge(f_free, 5 * p + 5)
                            if j == 2:
                                pe.wait_ge(tr_kept, 12 * p + 4)
                            for c in range(NC):
                                mm = pe.transpose(banks[4 - 2 * (j % 2) + c // 4][0:C, (c % 4) * P:(c % 4 + 1) * P], src[:, cut(c)],
                                                  keep["eye"][:, :])
                            mm.then_inc(tr_made, 1)
                        pe.wait_ge(tr_kept, 12 * p + 8)
                    keys = None
                    for i in range(len(INV_LEVELS)):
                        if p < PAIRS:
                            pe.wait_ge(x_made, 5 * p + i + 1)
                            pe.wait_ge(c_ready, 5 * p + i + 1)
                            if 5 * p + i:
                                pe.wait_ge(cx_kept, 5 * p + i)
                            products(2, ct, xx, cx_made)
                        if p and i == 0:
                            pe.wait_ge(y_kept, p)
                            whole("mean", p, bones[:, :], y_all[:, p - 1, :], mean_made)
                        if i == 0 and p + 1 < PAIRS:
                            keys = ws.blocks(pe, claim("k", p + 1), hh, hl)
                        if keys:
                            next(keys, None)
                        if p and i == 2:
                            pe.wait_ge(ysq_made, p)
                            whole("var", p, bones[:, :], yq[:, :], var_made)
                        if p < PAIRS:
                            pe.wait_ge(cx_kept, 5 * p + i + 1)
                            pe.wait_ge(xt_made, 6 * p + i + 1)
                            if i == 0:
                                pe.wait_ge(tr_kept, 12 * p + 12)
                            if i < len(INV_LEVELS) - 1:
                                products(5, xt, pp, xcx_made)
                            products(4, pp, xt, xcxt_made)
                        if keys:
                            next(keys, None)

            @block.scalar
            def _(act):
                st = Steps(act, own_a)

                def copy_out(name, p, f, n):
                    act.wait_ge(ws.used, n + 1)
                    if f >= 2:
                        act.wait_ge(z_free, f - 1)
                    e = place[name, p]
                    st.settle()
                    st.do(act.activation(z[:, f % 2, 1:S + 1], banks[e % 2][:, :], ACT.Copy), read(name, p))

                def post(p, part):
                    if part == 0:
                        act.wait_ge(*read("mean", p))
                        st.settle()
                        st.do(act.activation(yq[:, :], y_all[:, p - 1, :], ACT.Square), (ysq_made, p))
                    else:
                        act.wait_ge(var_made, p)
                        st.settle()
                        st.do(act.activation(yq[:, :], banks[place["var", p] % 2][:, :], ACT.Ln, scale=1.0 / C,
                                             bias=keep["eps"][:, 2:3]), read("var", p))
                        st.settle()
                        st.do(act.activation(yq[:, :], yq[:, :], ACT.Exp, scale=-0.5), (yr_made, p))

                act.wait_ge(par_made, 1)
                for n in range(3):
                    ws.high(st, n + 1)
                    copy_out("low", n, n, n)
                act.wait_ge(z_free, 1)
                st.settle()
                st.do(act.activation(wa[0:64, :], wa[0:64, :], ACT.Tanh), (wa_made, 1))
                for i in range(2):
                    act.wait_ge(z_free, 2 + i)
                    sigmoid_steps(st, gd[:, i, :], gd[:, i, :], (gd_made, i + 1), half)
                for p in range(PAIRS + 1):
                    if p < PAIRS:
                        n, f = 3 + 3 * p, 3 + 3 * p
                        if p == 0:
                            ws.high(st, n + 1)
                        copy_out("k", p, f, n)
                        act.wait_ge(lr_made, 2 * p + 1)
                        if p:
                            act.wait_ge(c_made, p)
                        sigmoid_steps(st, lw[:, :], banks[place["w", p] % 2][:, :], (wsig, p + 1), half, bias=halves[:, p:p + 1],
                                      free=read("w", p))
                        act.wait_ge(lr_made, 2 * p + 2)
                        if p:
                            act.wait_ge(f_made, 5 * p)
                            act.wait_ge(bbar_made, p)
                        sigmoid_steps(st, a[:, :], banks[place["a", p] % 2][:, :], (asig, p + 1), half,
                                      bias=halves[:, 8 + p:9 + p], free=read("a", p))
                        if p:
                            act.wait_ge(tr_made, 3 * p)
                        act.wait_ge(z_free, f + 1)
                        st.settle()
                        st.do(act.activation(e0[:, :], ks[:, :], ACT.Square, scale=col("k_k", p)), (sq_made, p + 1))
                        ws.high(st, n + 2)
                        act.wait_ge(b_made, p + 1)
                        st.settle()
                        st.do(act.activation(e1[:, :], cum[:, :], ACT.Exp, scale=-1.0), (enb_made, p + 1))
                        act.wait_ge(c_made, p + 1)
                        st.settle()
                        st.do(act.activation(lw[:, :], lw[:, :], ACT.Exp), (ebm_made, p + 1))
                        copy_out("r", p, f + 1, n + 1)
                        act.wait_ge(ssq_made, p + 1)
                        st.settle()
                        st.do(act.activation(e0[:, :], cum[:, :], ACT.Exp), (eb_made, p + 1))
                        ws.high(st, n + 3)
                        act.wait_ge(*read("ssq", p))
                        st.settle()
                        st.do(act.activation(kn[:, :], kn[:, :], ACT.Ln, scale=2.0 ** 20))
                        st.settle()
                        st.do(act.activation(kn[:, :], kn[:, :], ACT.Exp, scale=-0.5, bias=keep["eps"][:, 1:2]),
                              (rn_made, p + 1))
                        copy_out("v", p, f + 2, n + 2)
                        ws.high(st, n + 4)
                        act.wait_ge(g_made, p + 1)
                        if p >= 2:
                            act.wait_ge(y_done, p - 1)
                        st.settle()
                        st.do(act.activation(gg[:, p % 2, :], banks[place["g", p] % 2][:, :], ACT.Copy), read("g", p))
                    if p:
                        act.wait_ge(ch_made, 24 * p)
                        st.settle()
                        st.do(act.activation(y_all[:, p - 1, :], banks[7][:, :], ACT.Copy), (y_kept, p))
                    if p < PAIRS:
                        for j, dst in enumerate((vt, bt, ktt)):
                            act.wait_ge(tr_made, 3 * p + j + 1)
                            for i in range(4):
                                g, h = i // 2, i % 2
                                src = banks[4 - 2 * (j % 2) + g][0:C, :].rearrange("p (c h k) -> p c h k", c=4, h=2)[:, :, h, :]
                                out = dst[h * C:(h + 1) * C, g * 256:(g + 1) * 256].rearrange("p (c k) -> p c k", c=4)
                                st.settle()
                                st.do(act.activation(out, src, ACT.Copy), (tr_kept, 12 * p + 4 * j + i + 1))
                    for i in range(len(INV_LEVELS)):
                        if p < PAIRS:
                            act.wait_ge(cx_made, 5 * p + i + 1)
                            if 5 * p + i:
                                act.wait_ge(xcxt_made, 5 * p + i)
                            st.settle()
                            st.do(act.activation(pp[:, :], banks[2][:, :], ACT.Copy), (cx_kept, 5 * p + i + 1))
                        if p and i in (0, 2):
                            post(p, i // 2)

            @block.vector
            def _(dve):
                st = Steps(dve, own_v)

                def do(ins, signal=None):
                    st.do(ins, signal)
                    st.settle()

                def chain(p, i):
                    n = 24 * p + i
                    dve.wait_ge(ch_made, n + 1)
                    done = (ch_kept, n + 2)
                    if i % 3 == 0:
                        do(dve.tensor_copy(rhs[:, :], banks[6][:, 0:C]), done)
                    elif i % 3 == 1:
                        do(dve.tensor_copy(uu[:, :], banks[6][:, C:2 * C]), done)
                    elif i < 23:
                        c = i // 3
                        do(dve.scalar_tensor_tensor(out=state[:, :], in0=state[:, :], scalar=ec[:, p % 2, c:c + 1],
                                                    in1=banks[6][:, 2 * C:3 * C], op0=ALU.mult, op1=ALU.add), done)
                    else:
                        do(dve.memset(state[:, :], 0.0), done)

                def shift(f, name, p, dst, mu):
                    dve.wait_ge(*read(name, p))
                    do(dve.tensor_tensor(dst, z[:, f % 2, 0:S], z[:, f % 2, 1:S + 1], ALU.subtract))
                    do(dve.scalar_tensor_tensor(out=dst, in0=dst, scalar=mu, in1=z[:, f % 2, 1:S + 1],
                                                op0=ALU.mult, op1=ALU.add), (z_free, f + 1))

                dve.wait_ge(par_in, 16)
                do(dve.memset(z[:, :, 0:1], 0.0))
                do(dve.tensor_scalar(halves[:, 0:8], par[:, B_AT["w0"][0]:B_AT["w0"][1]], 0.5, None, ALU.mult))
                do(dve.tensor_scalar(halves[:, 8:16], par[:, B_AT["a0"][0]:B_AT["a0"][1]], 0.5, None, ALU.mult),
                   (par_made, 1))
                do(dve.memset(state[:, :], 0.0), (ch_kept, 1))
                shift(0, "low", 0, wa[:, :], col("mu_wa", 0))
                shift(1, "low", 1, gd[:, 0, :], col("mu_g", 0))
                shift(2, "low", 2, gd[:, 1, :], col("mu_g", 1))
                dve.wait_ge(const_in, 48)
                for p in range(PAIRS + 1):
                    def step(*which):
                        if p:
                            for i in which:
                                chain(p - 1, i)
                    if p == PAIRS:
                        step(*range(24))
                    else:
                        f, b2 = 3 + 3 * p, p % 2
                        shift(f, "k", p, ks[:, :], col("mu_k", p))
                        step(0, 1)
                        dve.wait_ge(wsig, p + 1)
                        do(dve.tensor_scalar(lw[:, :], lw[:, :], -float(np.exp(-0.5)), None, ALU.mult))
                        step(2)
                        do(dve.tensor_tensor_scan(cum[:, :], reset[:, :], lw[:, :], 0.0, ALU.mult, ALU.add),
                           (b_made, p + 1))
                        step(3)
                        do(dve.tensor_tensor(lw[:, :], cum[:, :], lw[:, :], ALU.subtract), (c_made, p + 1))
                        step(4)
                        dve.wait_ge(asig, p + 1)
                        do(dve.tensor_scalar(kp[:, :], a[:, :], 1.0, col("k_a", p), ALU.subtract, ALU.mult))
                        step(5)
                        do(dve.scalar_tensor_tensor(out=kp[:, :], in0=kp[:, :], scalar=1.0, in1=ks[:, :],
                                                    op0=ALU.add, op1=ALU.mult))
                        step(*range(6, 11))
                        dve.wait_ge(ssq_made, p + 1)
                        do(dve.tensor_scalar(kn[:, :], banks[place["ssq", p] % 2][:, :], 1e-24, None, ALU.max),
                           read("ssq", p))
                        step(11)
                        shift(f + 1, "r", p, r[:, :], col("mu_r", p))
                        step(12, 13, 14, 15)
                        dve.wait_ge(rn_made, p + 1)
                        do(dve.scalar_tensor_tensor(out=kn[:, :], in0=ks[:, :], scalar=col("k_k", p), in1=kn[:, :],
                                                    op0=ALU.mult, op1=ALU.mult))
                        do(dve.tensor_tensor(a[:, :], kn[:, :], a[:, :], ALU.mult))
                        step(16)
                        dve.wait_ge(enb_made, p + 1)
                        do(dve.tensor_tensor(a[:, :], a[:, :], e1[:, :], ALU.mult))
                        step(17)
                        if p:
                            dve.wait_ge(f_made, 5 * p)
                        do(dve.tensor_tensor(kt[:, :], kp[:, :], e1[:, :], ALU.mult))
                        step(18)
                        dve.wait_ge(ebm_made, p + 1)
                        do(dve.scalar_tensor_tensor(out=at_[:, b2, :], in0=kn[:, :], scalar=-1.0, in1=lw[:, :],
                                                    op0=ALU.mult, op1=ALU.mult))
                        step(19)
                        dve.wait_ge(eb_made, p + 1)
                        do(dve.tensor_tensor(rt[:, b2, :], r[:, :], e0[:, :], ALU.mult), (rt_made, p + 1))
                        step(20)
                        do(dve.scalar_tensor_tensor(out=r[:, :], in0=r[:, :], scalar=col("r_k", p), in1=kp[:, :],
                                                    op0=ALU.mult, op1=ALU.mult), (rk_made, p + 1))
                        step(21, 22, 23)
                        do(dve.tensor_copy(ec[:, b2, :], e0[:, C - 1:S:C]))
                        ends = ec[:, b2, :].unsqueeze(2).broadcast_to([P, NC, C])
                        do(dve.tensor_tensor(chunks(e0[:, :]), chunks(a[:, :]), ends, ALU.mult), (bbar_made, p + 1))
                        do(dve.tensor_tensor(chunks(e1[:, :]), chunks(kt[:, :]), ends, ALU.mult), (kbar_made, p + 1))
                        if p:
                            dve.wait_ge(tr_made, 3 * p)
                        shift(f + 2, "v", p, v[:, :], col("mu_v", p))

                        def keep_masked(j):
                            dst, m = ((mabt, 0), (xx, 2), (mak, 0), (mrb, 1), (mrk, 1))[j]
                            dve.wait_ge(f_made, 5 * p + j + 1)
                            if j == 1 and p:
                                dve.wait_ge(xcxt_made, 5 * p)
                            do(dve.tensor_tensor(chunks(dst[:, :]), chunks(banks[2 + j % 2][:, :]),
                                                 each_chunk(lm[:, m, :]), ALU.mult), (f_free, 5 * p + j + 1))
                        keep_masked(0)
                        dve.wait_ge(bon_made, p + 1)
                        do(dve.tensor_tensor(bonus[:, b2, :], banks[place["bonus", p] % 2][:, :], v[:, :], ALU.mult),
                           read("bonus", p))
                        for j in range(1, 5):
                            keep_masked(j)
                        one = each_chunk(lm[:, 9, :])
                        do(dve.tensor_tensor(chunks(xx[:, :]), chunks(xx[:, :]), one, ALU.add), (x_made, 5 * p + 1))
                        do(dve.tensor_tensor(chunks(ct[:, :]), chunks(mabt[:, :]), each_chunk(lm[:, 4, :]), ALU.mult),
                           (c_ready, 5 * p + 1))
                        do(dve.tensor_tensor(chunks(xt[:, :]), chunks(mabt[:, :]), each_chunk(lm[:, 3, :]), ALU.mult))
                        do(dve.tensor_tensor(chunks(xt[:, :]), chunks(xt[:, :]), one, ALU.add), (xt_made, 6 * p + 1))
                    for i in range(len(INV_LEVELS)):
                        if p and i == 0:
                            dve.wait_ge(mean_made, p)
                            y = y_all[:, p - 1, :]
                            do(dve.scalar_tensor_tensor(out=y, in0=banks[place["mean", p] % 2][:, :], scalar=-1.0 / C,
                                                        in1=y, op0=ALU.mult, op1=ALU.add), read("mean", p))
                        if p < PAIRS:
                            if i < len(INV_LEVELS) - 1:
                                dve.wait_ge(xcx_made, 4 * p + i + 1)
                                do(dve.tensor_tensor(xx[:, :], xx[:, :], banks[5][:, :], ALU.add), (x_made, 5 * p + i + 2))
                                do(dve.tensor_tensor(chunks(ct[:, :]), chunks(mabt[:, :]), each_chunk(lm[:, 5 + i, :]),
                                                     ALU.mult), (c_ready, 5 * p + i + 2))
                            dve.wait_ge(xcxt_made, 5 * p + i + 1)
                            do(dve.tensor_tensor(xt[:, :], xt[:, :], banks[4][:, :], ALU.add), (xt_made, 6 * p + i + 2))
                        if p and i == 3:
                            y, j = y_all[:, p - 1, :], (p - 1) % 2
                            dve.wait_ge(yr_made, p)
                            do(dve.tensor_tensor(y, y, yq[:, :], ALU.mult))
                            do(dve.tensor_scalar(y, y, col("gn_w", p - 1), col("gn_b", p - 1), ALU.mult, ALU.add))
                            do(dve.tensor_tensor(y, y, bonus[:, j, :], ALU.add))
                            do(dve.tensor_tensor(y, y, gg[:, j, :], ALU.mult), (y_done, p))
        sc.clear()


class PostNorm:

    def __init__(self, sc, y, sq, acc, rstd):
        self.y, self.sq, self.acc, self.rstd = y, sq, acc, rstd
        self.sq_made, self.sq_used = sc.sem("pn_sq_made"), sc.sem("pn_sq_used")
        self.sum_made, self.rstd_made = sc.sem("pn_sum_made"), sc.sem("pn_rstd_made")

    def act_rstd(self, st, bank, eps_col):
        st.do(st.eng.activation(self.rstd[:, 0:1], eps_col, ACT.Ln))
        st.eng.wait_ge(self.sum_made, 1)
        st.settle()
        st.do(st.eng.activation(self.rstd[:, :], bank[:, :], ACT.Ln, scale=1.0 / D, bias=eps_col))
        st.settle()
        st.do(st.eng.activation(self.rstd[:, :], self.rstd[:, :], ACT.Exp, scale=-0.5), (self.rstd_made, 1))

    def dve_sum(self, st, k):
        st.eng.wait_ge(self.sq_made, k + 1)
        st.settle()
        if k == 0:
            ins = st.eng.tensor_copy(self.acc[:, :], self.sq[:, 0, :])
        else:
            ins = st.eng.tensor_tensor(self.acc[:, :], self.acc[:, :], self.sq[:, k % 2, :], ALU.add)
        st.do(ins, (self.sq_used, k + 1))

    def dve_add(self, st, x, w):
        st.eng.wait_ge(self.rstd_made, 1)
        for k in range(KD):
            st.settle()
            st.do(st.eng.tensor_tensor(self.y[:, k, :], self.y[:, k, :], self.rstd[:, :], ALU.mult))
            st.settle()
            st.do(st.eng.scalar_tensor_tensor(out=x[:, k, :], in0=self.y[:, k, :], scalar=w[:, k:k + 1],
                                              in1=x[:, k, :], op0=ALU.mult, op1=ALU.add))

    def pe(self, pe, bank, ones):
        pe.wait_ge(self.sq_used, KD)
        pe.matmul(bank[:, :], ones[:, :], self.acc[:, :], start=True, stop=True).then_inc(self.sum_made, 1)


def mix_b(nc, io, keep, l, hh, hl, mixed, y_all):
    with ExitStack() as ctx:
        sc = Scope(nc, ctx, "mx")
        x = keep["x"]
        half = keep["eps"][:, 3:4]
        banks = [sc.ps(f"bank{i}", [P, 512]) for i in range(8)]
        par = sc.sb("par", [P, B_N])
        units = []
        for n in range(KD):
            units += [(io["b_wgb"][l, n], D), (io["b_wor"][l, n], D)]
        units += [(io["b_wout"][l, n], D) for n in range(KD)]
        ws = Weights(sc, units)
        yh, yl = sc.sb("y_hi", [P, KD, S], F32R), sc.sb("y_lo", [P, KD, S], F32R)
        mh, ml = sc.sb("m_hi", [P, KD, S], F32R), sc.sb("m_lo", [P, KD, S], F32R)
        sig, sq = sc.sb("sig", [P, 2, S]), sc.sb("sq", [P, 2, S])
        acc, rstd = sc.sb("acc", [P, S]), sc.sb("rstd", [P, S])
        pn = PostNorm(sc, y_all, sq, acc, rstd)
        par_in, sig_made, g_free, y_free = sc.sem("par_in"), sc.sem("sig_made"), sc.sem("g_free"), sc.sem("y_free")
        yh_made, yl_made, mh_made, ml_made, z_made = (sc.sem("yh_made"), sc.sem("yl_made"), sc.sem("mh_made"),
                                                      sc.sem("ml_made"), sc.sem("z_made"))
        m_made = sc.sem("m_made")
        own_a, own_v, own_p = sc.sem("own_a"), sc.sem("own_v"), sc.sem("own_p")
        with nc.Block() as block:
            @block.sync
            def _(sp):
                sp.dma_start(par[:, :], io["b_par"][l]).then_inc(par_in, 16)
                for n in range(len(units)):
                    ws.load(sp, n)

            @block.gpsimd
            def _(pool):
                st = Steps(pool, own_p)
                for n in range(len(units)):
                    ws.low(st, n)

            @block.scalar
            def _(act):
                st = Steps(act, own_a)
                ws.high(st, 0)
                for m in range(KD):
                    ws.high(st, 2 * m + 1)
                    act.wait_ge(ws.used, 2 * m + 1)
                    if m >= 2:
                        act.wait_ge(m_made, m - 1)
                    sigmoid_steps(st, sig[:, m % 2, :], banks[m % 2][:, :], (sig_made, m + 1), half, free=(g_free, m + 1))
                    ws.high(st, 2 * m + 2)
                ws.high(st, 17)
                for m in range(KD):
                    ws.high(st, min(16 + m + 1, 23))
                    act.wait_ge(z_made, m + 1)
                    if m >= 2:
                        act.wait_ge(pn.sq_used, m - 1)
                    st.settle()
                    st.do(act.activation(sq[:, m % 2, :], y_all[:, m, :], ACT.Square), (pn.sq_made, m + 1))
                pn.act_rstd(st, banks[6], keep["eps"][:, 0:1])

            @block.tensor
            def _(pe):
                for m in range(KD):
                    if m >= 2:
                        pe.wait_ge(g_free, m - 1)
                    ws.project(pe, banks[m % 2][:, :], hh, hl)
                    if m >= 2:
                        pe.wait_ge(y_free, m - 1)
                    ws.project(pe, banks[2 + m % 2][:, :], yh, yl, ready=yl_made if m == 0 else None)
                for m in range(KD):
                    if m >= 2:
                        pe.wait_ge(z_made, m - 1)
                    ws.project(pe, banks[4 + m % 2][:, :], mh, ml, ready=ml_made if m == 0 else None)
                pn.pe(pe, banks[6], keep["ones"])

            @block.vector
            def _(dve):
                st = Steps(dve, own_v)
                for k in range(KD):
                    st.settle()
                    st.do(dve.tensor_copy(yh[:, k, :], y_all[:, k, :]))
                    st.settle()
                    st.do(dve.tensor_tensor(yl[:, k, :], y_all[:, k, :], yh[:, k, :].bitcast(F32), ALU.subtract),
                          (yl_made, k + 1))
                for m in range(KD):
                    dve.wait_ge(sig_made, m + 1)
                    dve.wait_ge(ws.used, 2 * m + 2)
                    st.settle()
                    st.do(dve.tensor_tensor(sig[:, m % 2, :], sig[:, m % 2, :], banks[2 + m % 2][:, :], ALU.mult),
                          (y_free, m + 1))
                    st.settle()
                    st.do(dve.tensor_tensor(mixed[:, m, :], mixed[:, m, :], sig[:, m % 2, :], ALU.add), (m_made, m + 1))
                    st.settle()
                    st.do(dve.tensor_copy(mh[:, m, :], mixed[:, m, :]))
                    st.settle()
                    st.do(dve.tensor_tensor(ml[:, m, :], mixed[:, m, :], mh[:, m, :].bitcast(F32), ALU.subtract),
                          (ml_made, m + 1))
                dve.wait_ge(par_in, 16)
                for m in range(KD):
                    dve.wait_ge(ws.used, 16 + m + 1)
                    st.settle()
                    st.do(dve.tensor_copy(y_all[:, m, :], banks[4 + m % 2][:, :]), (z_made, m + 1))
                    if m:
                        pn.dve_sum(st, m - 1)
                pn.dve_sum(st, KD - 1)
                pn.dve_add(st, x, par[:, B_AT["norm_mix_post"][0]:B_AT["norm_mix_post"][1]])
        sc.clear()


def ffn_b(nc, io, keep, l):
    with ExitStack() as ctx:
        sc = Scope(nc, ctx, "fb")
        x = keep["x"]
        half = keep["eps"][:, 3:4]
        banks = [sc.ps(f"bank{i}", [P, 512]) for i in range(8)]
        par = sc.sb("par", [P, B_N])
        col = b_columns(par)
        hh, hl = sc.sb("h_hi", [P, KD, S], F32R), sc.sb("h_lo", [P, KD, S], F32R)
        yh, yl = sc.sb("y_hi", [P, KF, S], F32R), sc.sb("y_lo", [P, KF, S], F32R)
        units = [(io["b_wup"][l, n], D) for n in range(2 * KF)] + down_units(io["b_wd"], l)
        ws = Weights(sc, units, raw=3)
        pad = S + 2
        work = sc.sb("work", [P, 4 * pad + 4 * S])
        a_in = work[:, 0:4 * pad].rearrange("p (b s) -> p b s", b=4)
        conv = work[:, 4 * pad:4 * pad + 4 * S].rearrange("p (b s) -> p b s", b=4)
        down = work[:, 0:KD * S].rearrange("p (b s) -> p b s", b=KD)
        y = sc.sb("y", [P, 2, S])
        norm = Norm(sc, hh, hl, conv[:, 0:2, :], conv[:, 2:4, :], a_in[:, 0:2, 0:S], a_in[:, 2, 0:S], a_in[:, 3, 0:S])
        par_in, a_made, conv_made, gelu_made = sc.sem("par_in"), sc.sem("a_made"), sc.sem("conv_made"), sc.sem("gelu_made")
        lo_made, z_made, pads_made = sc.sem("y_lo_made"), sc.sem("z_made"), sc.sem("pads_made")
        own_a, own_v, own_p = sc.sem("own_a"), sc.sem("own_v"), sc.sem("own_p")
        sq, acc, rstd = sc.sb("sq", [P, S]), sc.sb("acc", [P, S]), sc.sb("rstd", [P, S])
        sq_made, acc_made, sum_made, r_made = sc.sem("sq_made"), sc.sem("acc_made"), sc.sem("sum_made"), sc.sem("r_made")
        with nc.Block() as block:
            @block.sync
            def _(sp):
                sp.dma_start(par[:, :], io["b_par"][l]).then_inc(par_in, 16)
                for n in range(len(units)):
                    ws.load(sp, n)

            @block.gpsimd
            def _(pool):
                st = Steps(pool, own_p)
                norm.pool(st, ws)
                for n in range(2, len(units)):
                    ws.low(st, n)

            @block.scalar
            def _(act):
                st = Steps(act, own_a)
                norm.act_sums(st, x, banks[6], keep["eps"][:, 0:1], ws)
                act.wait_ge(par_in, 16)
                norm.act_affine(st, par[:, B_AT["norm_ffn_pre"][0]:B_AT["norm_ffn_pre"][1]], None)
                for n in range(2 * KF + 2):
                    if n < 2 * KF:
                        if n + 1 < 2 * KF:
                            ws.high(st, n + 1)
                        act.wait_ge(ws.used, n + 1)
                        if n >= 4:
                            act.wait_ge(conv_made, n - 3)
                        elif n == 0:
                            act.wait_ge(pads_made, 1)
                        st.settle()
                        st.do(act.activation(a_in[:, n % 4, 2:S + 2], banks[n % 2][:, :], ACT.Copy), (a_made, n + 1))
                    if n >= 2 and n % 2 == 0:
                        j = n // 2 - 1
                        act.wait_ge(conv_made, 2 * j + 1)
                        c = conv[:, (2 * j) % 4, :]
                        st.settle()
                        st.do(act.activation(c, c, ACT.Gelu_apprx_tanh, bias=col("conv_b", 2 * j)), (gelu_made, j + 1))
                ws.high(st, 2 * KF + 1)
                for m in range(KD):
                    ws.high(st, min(2 * KF + 3 * m + 3, len(units) - 1))
                    act.wait_ge(z_made, m + 1)
                    if m:
                        act.wait_ge(acc_made, m)
                    st.settle()
                    st.do(act.activation(sq[:, :], down[:, m, :], ACT.Square), (sq_made, m + 1))
                act.wait_ge(sum_made, 1)
                st.settle()
                st.do(act.activation(rstd[:, :], banks[6][:, :], ACT.Ln, scale=1.0 / D, bias=keep["eps"][:, 0:1]))
                st.settle()
                st.do(act.activation(rstd[:, :], rstd[:, :], ACT.Exp, scale=-0.5), (r_made, 1))

            @block.tensor
            def _(pe):
                norm.pe(pe, banks[6], keep["ones"])
                for n in range(2 * KF):
                    if n >= 2:
                        pe.wait_ge(a_made, n - 1)
                    ws.project(pe, banks[n % 2][:, :], hh, hl, ready=norm.ready if n == 0 else None)
                for m in range(KD):
                    if m >= 2:
                        pe.wait_ge(z_made, m - 1)
                    for part, k0 in enumerate(range(0, KF, KD)):
                        ws.project(pe, banks[4 + m % 2][:, :], yh, yl, k0=k0, first=part == 0, last=part == 2,
                                   ready=lo_made if m == 0 else None)
                pe.wait_ge(acc_made, KD)
                pe.matmul(banks[6][:, :], keep["ones"][:, :], acc[:, :], start=True, stop=True).then_inc(sum_made, 1)

            @block.vector
            def _(dve):
                st = Steps(dve, own_v)

                def do(ins, signal=None):
                    st.do(ins, signal)
                    st.settle()
                norm.dve_sums(st)
                norm.dve_normalise(st, x)
                dve.wait_ge(par_in, 16)
                dve.wait_ge(norm.f_h.free[0], KD)
                st.settle()
                do(dve.memset(a_in[:, :, 0:2], 0.0), (pads_made, 1))

                def finish(j):
                    dve.wait_ge(gelu_made, j + 1)
                    do(dve.scalar_tensor_tensor(out=y[:, j % 2, :], in0=conv[:, (2 * j + 1) % 4, :],
                                                scalar=col("conv_b", 2 * j + 1), in1=conv[:, (2 * j) % 4, :],
                                                op0=ALU.add, op1=ALU.mult))
                    do(dve.tensor_copy(yh[:, j, :], y[:, j % 2, :]))
                    do(dve.tensor_tensor(yl[:, j, :], y[:, j % 2, :], yh[:, j, :].bitcast(F32), ALU.subtract),
                       (lo_made, j + 1))

                for n in range(2 * KF):
                    b = n % 4
                    dve.wait_ge(a_made, n + 1)
                    do(dve.tensor_scalar(conv[:, b, :], a_in[:, b, 0:S], col("conv0", n), None, ALU.mult))
                    for j in (1, 2):
                        do(dve.scalar_tensor_tensor(out=conv[:, b, :], in0=a_in[:, b, j:j + S], scalar=col(f"conv{j}", n),
                                                    in1=conv[:, b, :], op0=ALU.mult, op1=ALU.add),
                           (conv_made, n + 1) if j == 2 else None)
                    if n >= 2 and n % 2 == 0:
                        finish(n // 2 - 1)
                finish(KF - 1)
                for m in range(KD):
                    dve.wait_ge(ws.used, 2 * KF + 3 * (m + 1))
                    do(dve.tensor_copy(down[:, m, :], banks[4 + m % 2][:, :]), (z_made, m + 1))
                    dve.wait_ge(sq_made, m + 1)
                    if m == 0:
                        do(dve.tensor_copy(acc[:, :], sq[:, :]), (acc_made, 1))
                    else:
                        do(dve.tensor_tensor(acc[:, :], acc[:, :], sq[:, :], ALU.add), (acc_made, m + 1))
                dve.wait_ge(r_made, 1)
                w = par[:, B_AT["norm_ffn_post"][0]:B_AT["norm_ffn_post"][1]]
                for k in range(KD):
                    do(dve.tensor_tensor(down[:, k, :], down[:, k, :], rstd[:, :], ALU.mult))
                    do(dve.scalar_tensor_tensor(out=x[:, k, :], in0=down[:, k, :], scalar=w[:, k:k + 1], in1=x[:, k, :],
                                                op0=ALU.mult, op1=ALU.add))
        sc.clear()


def ple_b(nc, io, keep, l):
    with ExitStack() as ctx:
        sc = Scope(nc, ctx, "pl")
        x = keep["x"]
        half = keep["eps"][:, 3:4]
        banks = [sc.ps(f"bank{i}", [P, 512]) for i in range(8)]
        par = sc.sb("par", [P, B_N])
        xh, xl = sc.sb("x_hi", [P, KD, S], F32R), sc.sb("x_lo", [P, KD, S], F32R)
        ple = sc.sb("ple", [P, 2, S])
        ph, plo = sc.sb("p_hi", [P, 2, S], F32R), sc.sb("p_lo", [P, 2, S], F32R)
        units = [(io["b_wple"][l, n], D) for n in range(2)] + [(io["b_wpg"][l, n], D) for n in range(KD)]
        ws = Weights(sc, units)
        ge, sig, sq = sc.sb("ge", [P, KD, S]), sc.sb("sig", [P, 2, S]), sc.sb("sq", [P, 2, S])
        acc, rstd = sc.sb("acc", [P, S]), sc.sb("rstd", [P, S])
        pn = PostNorm(sc, ge, sq, acc, rstd)
        par_in, ple_in, pl_made, xl_made = sc.sem("par_in"), sc.sem("ple_in"), sc.sem("pl_made"), sc.sem("xl_made")
        e_made, e_kept, g_free, sig_made, ge_made = (sc.sem("e_made"), sc.sem("e_kept"), sc.sem("g_free"),
                                                     sc.sem("sig_made"), sc.sem("ge_made"))
        own_a, own_v, own_p = sc.sem("own_a"), sc.sem("own_v"), sc.sem("own_p")

        def e_done(m):
            return (ws.used, m // 4 + 1) if m % 4 == 3 else (e_made, m - m // 4 + 1)

        def square(st, m):
            st.eng.wait_ge(ge_made, m + 1)
            if m >= 2:
                st.eng.wait_ge(pn.sq_used, m - 1)
            st.settle()
            st.do(st.eng.activation(sq[:, m % 2, :], ge[:, m, :], ACT.Square), (pn.sq_made, m + 1))

        with nc.Block() as block:
            @block.sync
            def _(sp):
                sp.dma_start(ple[:, :, :], io["b_p"][l]).then_inc(ple_in, 16)
                sp.dma_start(par[:, :], io["b_par"][l]).then_inc(par_in, 16)
                for n in range(len(units)):
                    ws.load(sp, n)

            @block.gpsimd
            def _(pool):
                st = Steps(pool, own_p)
                for n in range(len(units)):
                    ws.low(st, n)

            @block.scalar
            def _(act):
                st = Steps(act, own_a)
                ws.high(st, 1)
                for m in range(KD):
                    act.wait_ge(*e_done(m))
                    st.settle()
                    st.do(act.activation(ge[:, m, :], banks[m % 2][:, :], ACT.Copy), (e_kept, m + 1))
                    if m == 3:
                        ws.high(st, 2)
                for m in range(KD):
                    ws.high(st, min(3 + m, len(units) - 1))
                    act.wait_ge(ws.used, 3 + m)
                    if m >= 2:
                        act.wait_ge(ge_made, m - 1)
                    sigmoid_steps(st, sig[:, m % 2, :], banks[2 + m % 2][:, :], (sig_made, m + 1), half, free=(g_free, m + 1))
                    if m:
                        square(st, m - 1)
                square(st, KD - 1)
                pn.act_rstd(st, banks[6], keep["eps"][:, 0:1])

            @block.tensor
            def _(pe):
                pe.wait_ge(pl_made, 2)
                for n in range(2):
                    s = ws.take(pe)
                    for j in range(4):
                        m = 4 * n + j
                        if m >= 2:
                            pe.wait_ge(e_kept, m - 1)
                        out = banks[m % 2][:, :]
                        for k in range(2):
                            a = slice((2 * j + k) * P, (2 * j + k + 1) * P)
                            pe.matmul(out, ws.hi[:, s, a], ph[:, k, :], start=k == 0, stop=False)
                            pe.matmul(out, ws.hi[:, s, a], plo[:, k, :], start=False, stop=False)
                            mm = pe.matmul(out, ws.lo[:, s, a], ph[:, k, :], start=False, stop=k == 1)
                        mm.then_inc(e_done(m)[0], 1)
                for m in range(KD):
                    if m >= 2:
                        pe.wait_ge(g_free, m - 1)
                    ws.project(pe, banks[2 + m % 2][:, :], xh, xl, ready=xl_made if m == 0 else None)
                pn.pe(pe, banks[6], keep["ones"])

            @block.vector
            def _(dve):
                st = Steps(dve, own_v)

                def do(ins, signal=None):
                    st.do(ins, signal)
                    st.settle()
                dve.wait_ge(ple_in, 16)
                do(dve.tensor_copy(ph[:, :, :], ple[:, :, :]), (pl_made, 1))
                do(dve.tensor_tensor(plo[:, :, :], ple[:, :, :], ph[:, :, :].bitcast(F32), ALU.subtract), (pl_made, 2))
                for k in range(KD):
                    do(dve.tensor_copy(xh[:, k, :], x[:, k, :]))
                    do(dve.tensor_tensor(xl[:, k, :], x[:, k, :], xh[:, k, :].bitcast(F32), ALU.subtract), (xl_made, k + 1))
                dve.wait_ge(par_in, 16)
                for m in range(KD):
                    dve.wait_ge(sig_made, m + 1)
                    do(dve.tensor_tensor(ge[:, m, :], ge[:, m, :], sig[:, m % 2, :], ALU.mult), (ge_made, m + 1))
                    if m:
                        pn.dve_sum(st, m - 1)
                pn.dve_sum(st, KD - 1)
                pn.dve_add(st, x, par[:, B_AT["norm_ple"][0]:B_AT["norm_ple"][1]])
        sc.clear()


def layer_b(nc, io, keep, l):
    with ExitStack() as ctx:
        hh = ctx.enter_context(nc.sbuf_tensor("bh_hi", [P, KD, S], F32R))
        hl = ctx.enter_context(nc.sbuf_tensor("bh_lo", [P, KD, S], F32R))
        mixed = ctx.enter_context(nc.sbuf_tensor("mixed", [P, KD, S], F32))
        attention_b(nc, io, keep, l, hh, hl, mixed)
        y_all = ctx.enter_context(nc.sbuf_tensor("y_all", [P, KD, S], F32))
        rwkv_b(nc, io, keep, l, hh, hl, y_all)
        mix_b(nc, io, keep, l, hh, hl, mixed, y_all)
    ffn_b(nc, io, keep, l)
    ple_b(nc, io, keep, l)


def final_norm_a(nc, io, keep):
    with ExitStack() as ctx:
        sc = Scope(nc, ctx, "fn")
        x = keep["x"]
        bank = sc.ps("bank", [P, 512])
        w, sq, acc = sc.sb("w", [P, KD]), sc.sb("sq", [P, 2, S]), sc.sb("acc", [P, S])
        w_in, sq_made, sq_used, acc_made = sc.sem("w_in"), sc.sem("sq_made"), sc.sem("sq_used"), sc.sem("acc_made")
        sum_made, rstd_made, own_a, own_v = sc.sem("sum_made"), sc.sem("rstd_made"), sc.sem("own_a"), sc.sem("own_v")
        with nc.Block() as block:
            @block.sync
            def _(sp):
                sp.dma_start(w[:, :], io["final_w"]).then_inc(w_in, 16)

            @block.scalar
            def _(act):
                st = Steps(act, own_a)
                for k in range(KD):
                    if k >= 2:
                        act.wait_ge(sq_used, k - 1)
                    st.do(act.activation(sq[:, k % 2, :], x[:, k, :], ACT.Square), (sq_made, k + 1))
                act.wait_ge(sum_made, 1)
                st.do(act.activation(acc[:, :], bank[:, :], ACT.Ln, scale=1.0 / D, bias=keep["eps"][:, 0:1]))
                st.settle()
                st.do(act.activation(acc[:, :], acc[:, :], ACT.Exp, scale=-0.5), (rstd_made, 1))

            @block.vector
            def _(dve):
                st = Steps(dve, own_v)
                for k in range(KD):
                    dve.wait_ge(sq_made, k + 1)
                    st.settle()
                    if k == 0:
                        ins = dve.tensor_copy(acc[:, :], sq[:, 0, :])
                    else:
                        ins = dve.tensor_tensor(acc[:, :], acc[:, :], sq[:, k % 2, :], ALU.add)
                    st.do(ins, (sq_used, k + 1))
                dve.wait_ge(rstd_made, 1)
                dve.wait_ge(w_in, 16)
                for k in range(KD):
                    st.settle()
                    st.do(dve.scalar_tensor_tensor(out=x[:, k, :], in0=x[:, k, :], scalar=w[:, k:k + 1],
                                                   in1=acc[:, :], op0=ALU.mult, op1=ALU.mult))

            @block.tensor
            def _(pe):
                pe.wait_ge(sq_used, KD)
                pe.matmul(bank[:, :], keep["ones"][:, :], acc[:, :], start=True, stop=True).then_inc(sum_made, 1)
        sc.clear()


def store(nc, io, keep):
    with ExitStack() as ctx:
        sc = Scope(nc, ctx, "st")
        out_done = sc.sem("out_done")
        with nc.Block() as block:
            @block.sync
            def _(sp):
                sp.dma_start(io["out"], keep["x"][:, :, :]).then_inc(out_done, 16)
                sp.wait_ge(out_done, 16)
        sc.clear()


def program(nc, io):
    with ExitStack() as ctx:
        sc = Scope(nc, ctx, "keep")
        keep = {"x": sc.sb("x", [P, KD, S]), "c_raw": sc.sb("c_raw", [P, KD]), "c_act": sc.sb("c_act", [P, KD]),
                "mod_pre": sc.sb("mod_pre", [P, 16]), "mod": sc.sb("mod", [P, 32]), "ones": sc.sb("ones", [P, P]),
                "eye": sc.sb("eye", [P, P]), "eps": sc.sb("eps", [P, 4])}
        prologue(nc, io, keep)
        with nc.Fori(0, DEPTH) as l:
            mixer_a(nc, io, keep, l)
            ffn_a(nc, io, keep, l)
        final_norm_a(nc, io, keep)
        if "b_pos" in io:
            keep["b_cos"], keep["b_sin"] = sc.sb("b_cos", [P, S]), sc.sb("b_sin", [P, S])
            rope_tables(nc, io, keep)
            with nc.Fori(0, DEPTH) as l:
                layer_b(nc, io, keep, l)
        store(nc, io, keep)


def tiles(w):
    *b, k, n = w.shape
    v = w.reshape(*b, k // P, P, n // P, P)
    v = np.moveaxis(v, -2, -4)
    v = np.swapaxes(v, -3, -2)
    return np.ascontiguousarray(v).reshape(*b, n // P, P, k)


def token_units(w, cols):
    *b, k, n = w.shape
    v = w.reshape(*b, k * cols // (D * P), D // cols, P, cols)
    return np.ascontiguousarray(np.swapaxes(v, -3, -2)).reshape(*b, k * cols // (D * P), P, D)


def feature_cols(v):
    return np.ascontiguousarray(np.swapaxes(v.reshape(*v.shape[:-1], -1, P), -1, -2))


def constants_a():
    f = np.float32
    pos = np.arange(S, dtype=f)
    inv = f(10000.0) ** (-np.arange(0, P, 2, dtype=f) / f(P))
    ang = pos[None, :] * inv[:, None]
    c, s = np.cos(ang).astype(f), np.sin(ang).astype(f)
    cos, sin = np.concatenate([c, c]), np.concatenate([-s, s])
    lg = np.log(1.0 - 2.0 ** (-5.0 - np.arange(HEADS, dtype=np.float64)))
    rel = np.arange(S)[None, :] - np.arange(P)[:, None]
    decay = np.where(rel[None] >= 0, np.exp(lg[:, None, None] * np.maximum(rel, 0)[None]), 0.0) * P ** -0.5
    i = np.arange(P)
    masks = np.zeros((P, LEVELS, P), np.int32)
    for li in range(LEVELS):
        s2 = 2 << li
        same = i[:, None] // s2 == i[None, :] // s2
        masks[:, li] = same & (i[:, None] % s2 < s2 // 2) & (i[None, :] % s2 >= s2 // 2)
    reset = np.ones((P, S), f)
    reset[:, ::P] = 0.0
    return {"a_cos": cos, "a_sin": sin, "a_decay": np.ascontiguousarray(decay.transpose(1, 0, 2)).astype(f),
            "a_masks": masks, "a_reset": reset, "ones": np.ones((P, P), f), "eye": np.eye(P, dtype=f)}


def arrays_a(inp):
    w_in = inp["w_in"]
    wv = np.stack([token_units(w_in[:, :, 1024:1536], S), token_units(w_in[:, :, 3072:3584], S)], 1)
    order = []
    for names in ((0, 512, 1536), (2560, 2048, 3584)):
        for h in range(HEADS):
            order += [o // P + h for o in names]
    wh = tiles(w_in)[:, order].reshape(DEPTH, 2, 12, P, D)
    ada = tiles(inp["ada_w"])
    ada_b = feature_cols(inp["ada_b"])
    nxt = [(l + 1) % DEPTH for l in range(DEPTH)]
    gv = np.stack([tiles(inp["w_gate"]), tiles(inp["w_val"])], 2).reshape(DEPTH, 2 * KF, P, D)
    lb = feature_cols(inp["hgrn_lb_logits"])
    par = {"norm1": feature_cols(inp["norm1_w"]), "norm2": feature_cols(inp["norm2_w"]),
           "ret_w": feature_cols(inp["ret_norm_w"]), "hgrn_w": feature_cols(inp["hgrn_norm_w"]),
           "lb0": lb[[0, 0]], "lb1": lb[[1, 1]],
           "lsel": np.broadcast_to(np.arange(DEPTH, dtype=np.float32)[:, None, None], (DEPTH, P, 1)),
           "ada_b": ada_b[:, :, 16:], "ada_b_next": ada_b[nxt][:, :, :16],
           "conv0": feature_cols(inp["conv_w"][:, 0]), "conv1": feature_cols(inp["conv_w"][:, 1]),
           "conv2": feature_cols(inp["conv_w"][:, 2]), "conv_b": feature_cols(inp["conv_b"])}
    out = {"x": np.ascontiguousarray(inp["x"][0].T.reshape(KD, P, S).transpose(1, 0, 2)), "c": feature_cols(inp["c"])[0],
           "ada_first": ada[0, :16], "ada": np.concatenate([ada[:, 16:], ada[nxt][:, :16]], 1),
           "ada_b_first": np.ascontiguousarray(ada_b[0, :, :16]), "a_wv": wv, "a_wh": wh, "a_wo": tiles(inp["w_out"]),
           "a_wgv": gv, "a_wd": tiles(inp["w_down"]), "a_par": np.concatenate([par[n] for n in A_COLS], -1),
           "final_w": feature_cols(inp["final_norm_w"])}
    out.update(constants_a())
    return out


def kernel(**inputs):
    import concourse.bacc as bacc
    from concourse.bass_utils import run_bass_kernel_spmd as run

    nc = bacc.Bacc("TRN2", target_bir_lowering=False, num_devices=1)
    inp = {n: np.asarray(a) for n, a in inputs.items()}
    arrays = {f"in_{n}": np.ascontiguousarray(a) for n, a in layout(inp).items()}
    io = {n[3:]: nc.dram_tensor(n, a.shape, mybir.dt.from_np(a.dtype), kind="ExternalInput").ap()
          for n, a in arrays.items()}
    io["out"] = nc.dram_tensor("out_0", (P, KD, S), F32, kind="ExternalOutput").ap()
    program(nc, io)
    r = run(nc, [arrays], core_ids=[0])
    return np.ascontiguousarray(r.results[0]["out_0"].transpose(1, 0, 2).reshape(D, S).T)[None]


def constants_b():
    f = np.float32
    half = 32
    inv = f(10000.0) ** (-np.arange(half, dtype=f) / f(half))
    row = np.arange(P)
    freq = np.stack([inv[row % half], np.where(row % 64 < half, -1.0, 1.0)], 1).astype(f)
    i, j = np.arange(P)[:, None], np.arange(2 * P)[None, :]
    dist = i + P - j
    inside = (dist >= 0) & (dist < P)
    later = np.where(inside, 0.0, -1e30)
    first = np.where(inside & (j >= P), 0.0, -1e30)
    band = np.concatenate([first, later, later], 1).astype(f)
    s, t = np.arange(C)[:, None], np.arange(C)[None, :]
    level = {}
    for n in (1, 2, 4, 8, 16, 32):
        same = s // (2 * n) == t // (2 * n)
        level[n] = same & (s % (2 * n) < n) & (t % (2 * n) >= n)
    lm = [s < t, s <= t, level[1].T, level[1]] + [level[n] for n in INV_LEVELS] + [s == t]
    lm = np.stack([m.astype(f) for m in lm], 1)
    bones = (row[:, None] // 64 == row[None, :] // 64).astype(f)
    reset = np.ones((P, S), f)
    reset[:, ::C] = 0.0
    return {"b_freq": freq, "b_band": band, "b_lm": np.concatenate([lm, lm]), "b_bones": bones, "b_reset": reset}


def arrays_b(inp):
    g = {n[:-2]: a for n, a in inp.items() if n.endswith("_2")}
    w = g["w_in"]
    heads = [4 * (2 * kb + s) + m for kb in range(2) for m in range(4) for s in range(2)]
    cols = np.concatenate([np.arange(64 * h, 64 * h + 64) for h in heads])
    att_q, att_kv = 1024, 256
    at = att_q + 2 * att_kv
    rw = w[:, :, at:at + 3 * RW + 288]
    rkv = [tiles(rw[:, :, i * RW:(i + 1) * RW]) for i in (1, 0, 2)]
    low = np.concatenate([rw[:, :, 3 * RW:], np.zeros((DEPTH, D, 96), np.float32)], -1)
    mu = g["rw_mu"]
    g2 = np.concatenate([g["rw_g2"], np.zeros((DEPTH, 96, RW), np.float32)], 1)
    gates = w[:, :, at + 3 * RW + 288:]
    order = heads_order = np.array(heads)
    sink = np.repeat(g["att_sinks"][:, heads_order], 2, axis=-1)
    up = tiles(g["w_up"])
    inter = [h * KF + j for j in range(KF) for h in range(2)]
    par = {n: feature_cols(g[m]) for n, m in (
        ("w0", "rw_w0"), ("a0", "rw_a0"), ("k_k", "rw_k_k"), ("k_a", "rw_k_a"), ("gn_w", "rw_gn_w"), ("gn_b", "rw_gn_b"),
        ("norm_mix_pre", "norm_mix_pre"), ("norm_mix_post", "norm_mix_post"), ("norm_ffn_pre", "norm_ffn_pre"),
        ("norm_ffn_post", "norm_ffn_post"), ("norm_ple", "norm_ple"))}
    par["r_k"] = feature_cols(g["rw_r_k"].reshape(DEPTH, RW))
    for i, n in enumerate(("mu_r", "mu_k", "mu_v")):
        par[n] = feature_cols(mu[:, i * RW:(i + 1) * RW])
    par["mu_wa"] = feature_cols(mu[:, 3 * RW:3 * RW + 128])
    par["mu_g"] = feature_cols(np.concatenate([mu[:, 3 * RW + 128:], np.zeros((DEPTH, 96), np.float32)], -1))
    for i in range(3):
        par[f"conv{i}"] = feature_cols(g["conv_w"][:, i])[:, :, inter]
    par["conv_b"] = feature_cols(g["conv_b"])[:, :, inter]
    ple = g["w_ple"].reshape(DEPTH, 2, P, 2, 4, P)
    out = {
        "b_pos": np.broadcast_to(g["positions"].astype(np.int32), (P, S)),
        "b_wk": tiles(w[:, :, att_q:att_q + att_kv]), "b_wv": token_units(w[:, :, att_q + att_kv:at], 256),
        "b_wq": tiles(w[:, :, :att_q][:, :, cols]), "b_sink": np.broadcast_to(sink[:, None, :], (DEPTH, P, 32)),
        "b_wga": tiles(gates[:, :, :D]), "b_wgb": tiles(gates[:, :, D:]), "b_woa": tiles(g["w_o_att"][:, cols]),
        "b_wlow": tiles(low), "b_wrkv": np.stack(rkv, 2).reshape(DEPTH, 3 * PAIRS, P, D),
        "b_wlr": np.concatenate([g["rw_w2"], g["rw_a2"]], 1).reshape(DEPTH, P, PAIRS, P).transpose(0, 2, 1, 3),
        "b_wg2": g2.reshape(DEPTH, 2, P, PAIRS, P).transpose(0, 3, 2, 1, 4),
        "b_wor": tiles(g["w_o_rw"]), "b_wout": tiles(g["w_out"]), "b_wup": up[:, inter], "b_wd": tiles(g["w_down"]),
        "b_wple": ple.transpose(0, 3, 2, 4, 1, 5).reshape(DEPTH, 2, P, D), "b_wpg": tiles(g["w_ple_gate"]),
        "b_p": g["p"][:, 0].transpose(0, 2, 1).reshape(DEPTH, 2, P, S).transpose(0, 2, 1, 3),
        "b_par": np.concatenate([par[n] for n in B_COLS], -1),
    }
    out.update(constants_b())
    return out


def layout(inp):
    return {**arrays_a(inp), **arrays_b(inp)}
```
